# Optimizing a Trainium2 kernel written in Bass

```python
import math
import jax
import jax.numpy as jnp
from jax import lax
import numpy as np

D_MODEL = 1024
BATCH = 1
SEQ = 512
DEPTH = 1
DEC_BATCH = 1
DEC_SEQ = 64
PAST_LEN = 128

CHUNK = 64
MIX_WIDTH = D_MODEL
DA_HEADS = 4
DA_QK_DIM = 64
DA_V_DIM = 2 * DA_QK_DIM
DA_WIDTH = DA_HEADS * DA_V_DIM
DA_SCALE = DA_QK_DIM ** -0.5
HG_HEADS = 4
HG_EXPAND = 128
HG_WIDTH = MIX_WIDTH - DA_WIDTH
HG_V_DIM = HG_WIDTH // HG_HEADS
HG_K_WIDTH = HG_HEADS * HG_EXPAND
DA_QK_WIDTH = DA_HEADS * 2 * DA_QK_DIM
IN_WIDTH = 2 * DA_QK_WIDTH + DA_WIDTH + 2 * HG_K_WIDTH + 2 * HG_WIDTH
SPLIT_POINTS = (
    DA_QK_WIDTH,
    2 * DA_QK_WIDTH,
    2 * DA_QK_WIDTH + DA_WIDTH,
    2 * DA_QK_WIDTH + DA_WIDTH + HG_K_WIDTH,
    2 * DA_QK_WIDTH + DA_WIDTH + 2 * HG_K_WIDTH,
    2 * DA_QK_WIDTH + DA_WIDTH + 2 * HG_K_WIDTH + HG_WIDTH,
)
Q_BLOCK = 128
N_MEM = 256
MEM_HEADS = 4
MEM_HEAD_DIM = D_MODEL // MEM_HEADS
N_GROUPS = 4
EXPERTS_PER_GROUP = 8
N_EXPERTS = N_GROUPS * EXPERTS_PER_GROUP
TOP_K = 2
EXPERT_FF = 512
EXPERT_BLOCK = 128
EPS = 1e-5

kernel_name = "hybrid_diffattn_hgrn2_hmoe_stream_step"

def rms_norm(x, g):
    x32 = x.astype(jnp.float32)
    y = x32 * lax.rsqrt(jnp.mean(x32 * x32, axis=-1, keepdims=True) + EPS)
    return (y * g.astype(jnp.float32)).astype(x.dtype)

def lambda_init(layer):
    return 0.8 - 0.6 * math.exp(-0.3 * layer)

def alibi_slopes(n_heads):
    return jnp.exp2(-8.0 * jnp.arange(1, n_heads + 1, dtype=jnp.float32) / n_heads)

def _diff_attn_core(q, k, v, q_pos, k_pos, lam):
    s = jnp.einsum("bqhcd,bkhcd->bchqk", q, k, preferred_element_type=jnp.float32) * DA_SCALE
    dist = jnp.abs(q_pos[:, None] - k_pos[None, :]).astype(jnp.float32)
    bias = -alibi_slopes(DA_HEADS)[:, None, None] * dist
    visible = (k_pos[None, :] // CHUNK) <= (q_pos[:, None] // CHUNK)
    s = jnp.where(visible, s + bias, -jnp.inf)
    p = jax.nn.softmax(s, axis=-1)
    w = p[:, 0] - lam * p[:, 1]
    return jnp.einsum("bhqk,bkhd->bqhd", w, v.astype(jnp.float32))

def diff_attention(q, k, v, q_pos, k_pos, lam):
    B, T = q.shape[0], q.shape[1]
    if T > Q_BLOCK and T % Q_BLOCK == 0:
        n = T // Q_BLOCK
        qb = jnp.moveaxis(q.reshape(B, n, Q_BLOCK, *q.shape[2:]), 1, 0)
        pb = q_pos.reshape(n, Q_BLOCK)
        ob = lax.map(lambda a: _diff_attn_core(a[0], k, v, a[1], k_pos, lam), (qb, pb))
        return jnp.moveaxis(ob, 0, 1).reshape(B, T, *ob.shape[3:])
    return _diff_attn_core(q, k, v, q_pos, k_pos, lam)

def hgrn2_chunkwise(q, k, log_f, v, s0, block):
    B, T, H, DK = q.shape
    DV = v.shape[-1]
    n = T // block

    def to_blocks(a):
        return a.reshape(B, n, block, H, a.shape[-1]).transpose(1, 0, 3, 2, 4)

    causal = jnp.tril(jnp.ones((block, block), dtype=bool))[:, :, None]

    def step(s, inp):
        qc, kc, gc, vc = inp
        b = jnp.cumsum(gc, axis=2)
        rel = b[:, :, :, None, :] - b[:, :, None, :, :]
        decay = jnp.exp(jnp.where(causal, rel, -jnp.inf))
        scores = jnp.einsum("bhtd,bhsd,bhtsd->bhts", qc, kc, decay)
        o = (jnp.einsum("bhts,bhsv->bhtv", scores, vc)
             + jnp.einsum("bhtd,bhdv->bhtv", qc * jnp.exp(b), s))
        b_last = b[:, :, -1:, :]
        s_new = (jnp.exp(b_last[:, :, 0, :])[..., None] * s
                 + jnp.einsum("bhsd,bhsv->bhdv", kc * jnp.exp(b_last - b), vc))
        return s_new, o

    s_fin, o = lax.scan(step, s0, (to_blocks(q), to_blocks(k), to_blocks(log_f), to_blocks(v)))
    return o.transpose(1, 0, 3, 2, 4).reshape(B, T, H, DV), s_fin

def grouped_experts(xf, e_idx, gate, w_gate, w_up, w_down):
    N, D = xf.shape
    K = e_idx.shape[1]
    M = N * K
    flat_e = e_idx.reshape(M).astype(jnp.int32)
    flat_tok = jnp.arange(M, dtype=jnp.int32) // K
    flat_w = gate.reshape(M)
    order = jnp.argsort(flat_e)
    se = flat_e[order]
    counts = jnp.bincount(flat_e, length=N_EXPERTS)
    padded = (counts + EXPERT_BLOCK - 1) // EXPERT_BLOCK * EXPERT_BLOCK
    pad_end = jnp.cumsum(padded)
    pad_start = pad_end - padded
    start = jnp.cumsum(counts) - counts
    dest = pad_start[se] + jnp.arange(M, dtype=jnp.int32) - start[se]
    n_blocks = (M + EXPERT_BLOCK - 1) // EXPERT_BLOCK + N_EXPERTS
    P = n_blocks * EXPERT_BLOCK
    row_tok = jnp.full((P,), N, jnp.int32).at[dest].set(flat_tok[order])
    row_w = jnp.zeros((P,), jnp.float32).at[dest].set(flat_w[order])
    blk_start = jnp.arange(n_blocks, dtype=jnp.int32) * EXPERT_BLOCK
    blk_e = jnp.minimum(jnp.searchsorted(pad_end, blk_start, side="right"), N_EXPERTS - 1)
    x_pad = jnp.concatenate([xf, jnp.zeros((1, D), xf.dtype)], axis=0)

    def one_block(args):
        toks, e = args
        xb = x_pad[toks]
        hb = jax.nn.silu(xb @ w_gate[e]) * (xb @ w_up[e])
        return hb @ w_down[e]

    yb = lax.map(one_block, (row_tok.reshape(n_blocks, EXPERT_BLOCK), blk_e))
    yb = yb.reshape(P, D) * row_w[:, None].astype(yb.dtype)
    return jnp.zeros((N + 1, D), yb.dtype).at[row_tok].add(yb)[:N]

def hier_moe(h, wg_r, bg_r, we_r, be_r, w_gate, w_up, w_down):
    B, T, D = h.shape
    xf = h.reshape(B * T, D)
    N = xf.shape[0]
    glog = (xf @ wg_r).astype(jnp.float32) + bg_r.astype(jnp.float32)
    gprob = jax.nn.softmax(glog, axis=-1)
    g_idx = jnp.argmax(glog, axis=-1).astype(jnp.int32)
    g_w = jnp.take_along_axis(gprob, g_idx[:, None], axis=-1)[:, 0]
    elog = ((xf @ we_r).astype(jnp.float32) + be_r.astype(jnp.float32)).reshape(N, N_GROUPS, EXPERTS_PER_GROUP)
    elog_g = jnp.take_along_axis(elog, g_idx[:, None, None], axis=1)[:, 0]
    top_v, top_i = lax.top_k(elog_g, TOP_K)
    gate = jax.nn.softmax(top_v, axis=-1) * g_w[:, None]
    e_idx = g_idx[:, None] * EXPERTS_PER_GROUP + top_i.astype(jnp.int32)
    y = grouped_experts(xf, e_idx, gate, w_gate, w_up, w_down)
    return y.reshape(B, T, D)

def memory_kv(mem, g, wk, wv):
    B = mem.shape[0]
    mn = rms_norm(mem, g)
    k = (mn @ wk).reshape(B, N_MEM, MEM_HEADS, MEM_HEAD_DIM)
    v = (mn @ wv).reshape(B, N_MEM, MEM_HEADS, MEM_HEAD_DIM)
    return k, v

def encoder_layer(x, past_len, past_k, past_v, s0, mem_k, mem_v, lw):
    B, T, _ = x.shape
    h = rms_norm(x, lw["ln_mix"])
    z = h @ lw["w_in"]
    dq, dk, dv, hq, hf, hi, hg = jnp.split(z, SPLIT_POINTS, axis=-1)
    k_rows = dk.reshape(B, T, DA_HEADS, 2 * DA_QK_DIM)
    v_rows = dv.reshape(B, T, DA_HEADS, DA_V_DIM)
    if past_k is None:
        k_all, v_all = k_rows, v_rows
    else:
        k_all = jnp.concatenate([past_k.astype(k_rows.dtype), k_rows], axis=1)
        v_all = jnp.concatenate([past_v.astype(v_rows.dtype), v_rows], axis=1)
    q_pos = past_len + jnp.arange(T, dtype=jnp.int32)
    k_pos = jnp.arange(past_len + T, dtype=jnp.int32)
    lp = lw["da_lambda"].astype(jnp.float32)
    lam = jnp.exp(jnp.sum(lp[0] * lp[1])) - jnp.exp(jnp.sum(lp[2] * lp[3])) + lw["lam_init"]
    o_da = diff_attention(dq.reshape(B, T, DA_HEADS, 2, DA_QK_DIM),
                          k_all.reshape(B, past_len + T, DA_HEADS, 2, DA_QK_DIM),
                          v_all, q_pos, k_pos, lam)
    o_da = rms_norm(o_da, lw["da_subln"]) * (1.0 - lw["lam_init"])
    lb = lw["hg_lb"]
    hf32 = hf.astype(jnp.float32)
    f = lb + (1.0 - lb) * jax.nn.sigmoid(hf32)
    kk = (1.0 - lb) * jax.nn.sigmoid(-hf32)
    log_f = jnp.log(f)
    qh = jax.nn.silu(hq.astype(jnp.float32))
    if s0 is None:
        s0 = jnp.zeros((B, HG_HEADS, HG_EXPAND, HG_V_DIM), jnp.float32)
    hshape = (B, T, HG_HEADS, HG_EXPAND)
    o_hg, s_new = hgrn2_chunkwise(qh.reshape(hshape), kk.reshape(hshape), log_f.reshape(hshape),
                                  hi.astype(jnp.float32).reshape(B, T, HG_HEADS, HG_V_DIM),
                                  s0.astype(jnp.float32), min(CHUNK, T))
    o_hg = rms_norm(o_hg, lw["hg_gnorm"]) * jax.nn.silu(hg.astype(jnp.float32)).reshape(B, T, HG_HEADS, HG_V_DIM)
    mixed = jnp.concatenate([o_da.reshape(B, T, DA_WIDTH), o_hg.reshape(B, T, HG_WIDTH)], axis=-1)
    x = x + mixed.astype(x.dtype) @ lw["w_out"]
    hm = rms_norm(x, lw["ln_mem"])
    qm = (hm @ lw["w_mem_q"]).reshape(B, T, MEM_HEADS, MEM_HEAD_DIM)
    sm = jnp.einsum("bthd,bmhd->bhtm", qm, mem_k.astype(qm.dtype),
                    preferred_element_type=jnp.float32) * (MEM_HEAD_DIM ** -0.5)
    pm = jax.nn.softmax(sm, axis=-1)
    om = jnp.einsum("bhtm,bmhd->bthd", pm, mem_v.astype(jnp.float32)).reshape(B, T, D_MODEL)
    x = x + om.astype(x.dtype) @ lw["w_mem_o"]
    x = x + hier_moe(rms_norm(x, lw["ln_ffn"]), lw["rg_w"], lw["rg_b"], lw["re_w"], lw["re_b"],
                     lw["e_gate"], lw["e_up"], lw["e_down"])
    return x, k_rows, v_rows, s_new.astype(x.dtype)

def setup_inputs(seed: int = 0) -> dict:
    key = jax.random.key(seed)
    ks = jax.random.split(key, 40)

    def nrm(k, shape, scale):
        return scale * jax.random.normal(k, shape, jnp.float32)

    return {
        "x_prompt": nrm(ks[0], (BATCH, SEQ, D_MODEL), 1.0),
        "x_sample": nrm(ks[1], (DEC_BATCH, DEC_SEQ, D_MODEL), 1.0),
        "mem_prompt": nrm(ks[2], (BATCH, N_MEM, D_MODEL), 1.0),
        "cache_diff_k": nrm(ks[3], (DEPTH, DEC_BATCH, PAST_LEN, DA_HEADS, 2 * DA_QK_DIM), 1.0),
        "cache_diff_v": nrm(ks[4], (DEPTH, DEC_BATCH, PAST_LEN, DA_HEADS, DA_V_DIM), 1.0),
        "state_hgrn": nrm(ks[5], (DEPTH, DEC_BATCH, HG_HEADS, HG_EXPAND, HG_V_DIM), 0.3),
        "cache_mem_k": nrm(ks[6], (DEPTH, DEC_BATCH, N_MEM, MEM_HEADS, MEM_HEAD_DIM), 1.0),
        "cache_mem_v": nrm(ks[7], (DEPTH, DEC_BATCH, N_MEM, MEM_HEADS, MEM_HEAD_DIM), 1.0),
        "ln_mix_g": 1.0 + nrm(ks[8], (DEPTH, D_MODEL), 0.02),
        "w_in": nrm(ks[9], (DEPTH, D_MODEL, IN_WIDTH), D_MODEL ** -0.5),
        "da_lambda": nrm(ks[10], (DEPTH, 4, DA_QK_DIM), 0.1),
        "da_subln_g": 1.0 + nrm(ks[11], (DEPTH, DA_V_DIM), 0.02),
        "hg_lb_logits": nrm(ks[12], (DEPTH + 1, HG_K_WIDTH), 0.5),
        "hg_gnorm_g": 1.0 + nrm(ks[13], (DEPTH, HG_V_DIM), 0.02),
        "w_out": nrm(ks[14], (DEPTH, MIX_WIDTH, D_MODEL), MIX_WIDTH ** -0.5),
        "ln_mem_g": 1.0 + nrm(ks[15], (DEPTH, D_MODEL), 0.02),
        "mem_norm_g": 1.0 + nrm(ks[16], (DEPTH, D_MODEL), 0.02),
        "w_mem_q": nrm(ks[17], (DEPTH, D_MODEL, D_MODEL), D_MODEL ** -0.5),
        "w_mem_k": nrm(ks[18], (DEPTH, D_MODEL, D_MODEL), D_MODEL ** -0.5),
        "w_mem_v": nrm(ks[19], (DEPTH, D_MODEL, D_MODEL), D_MODEL ** -0.5),
        "w_mem_o": nrm(ks[20], (DEPTH, D_MODEL, D_MODEL), D_MODEL ** -0.5),
        "ln_ffn_g": 1.0 + nrm(ks[21], (DEPTH, D_MODEL), 0.02),
        "router_group_w": nrm(ks[22], (DEPTH, D_MODEL, N_GROUPS), D_MODEL ** -0.5),
        "router_group_b": nrm(ks[23], (DEPTH, N_GROUPS), 0.01),
        "router_expert_w": nrm(ks[24], (DEPTH, D_MODEL, N_EXPERTS), D_MODEL ** -0.5),
        "router_expert_b": nrm(ks[25], (DEPTH, N_EXPERTS), 0.01),
        "exp_w_gate": nrm(ks[26], (DEPTH, N_EXPERTS, D_MODEL, EXPERT_FF), D_MODEL ** -0.5),
        "exp_w_up": nrm(ks[27], (DEPTH, N_EXPERTS, D_MODEL, EXPERT_FF), D_MODEL ** -0.5),
        "exp_w_down": nrm(ks[28], (DEPTH, N_EXPERTS, EXPERT_FF, D_MODEL), EXPERT_FF ** -0.5),
        "final_norm_g": 1.0 + nrm(ks[29], (D_MODEL,), 0.02),
    }

def reference(x_prompt, x_sample, mem_prompt, cache_diff_k, cache_diff_v, state_hgrn,
              cache_mem_k, cache_mem_v, ln_mix_g, w_in, da_lambda, da_subln_g, hg_lb_logits,
              hg_gnorm_g, w_out, ln_mem_g, mem_norm_g, w_mem_q, w_mem_k, w_mem_v, w_mem_o,
              ln_ffn_g, router_group_w, router_group_b, router_expert_w, router_expert_b,
              exp_w_gate, exp_w_up, exp_w_down, final_norm_g):
    lb_all = jnp.cumsum(jax.nn.softmax(hg_lb_logits.astype(jnp.float32), axis=0), axis=0)
    past_len = cache_diff_k.shape[2]
    yp, ys = x_prompt, x_sample
    kp_l, vp_l, sp_l, mkp_l, mvp_l, ks_l, vs_l, ss_l = [], [], [], [], [], [], [], []
    for l in range(DEPTH):
        lw = {
            "ln_mix": ln_mix_g[l], "w_in": w_in[l], "da_lambda": da_lambda[l],
            "da_subln": da_subln_g[l], "lam_init": lambda_init(l), "hg_lb": lb_all[l],
            "hg_gnorm": hg_gnorm_g[l], "w_out": w_out[l], "ln_mem": ln_mem_g[l],
            "w_mem_q": w_mem_q[l], "w_mem_o": w_mem_o[l], "ln_ffn": ln_ffn_g[l],
            "rg_w": router_group_w[l], "rg_b": router_group_b[l],
            "re_w": router_expert_w[l], "re_b": router_expert_b[l],
            "e_gate": exp_w_gate[l], "e_up": exp_w_up[l], "e_down": exp_w_down[l],
        }
        mk_p, mv_p = memory_kv(mem_prompt, mem_norm_g[l], w_mem_k[l], w_mem_v[l])
        yp, kp, vp, sp = encoder_layer(yp, 0, None, None, None, mk_p, mv_p, lw)
        ys, kss, vss, sss = encoder_layer(ys, past_len, cache_diff_k[l], cache_diff_v[l], state_hgrn[l],
                                          cache_mem_k[l], cache_mem_v[l], lw)
        kp_l.append(kp); vp_l.append(vp); sp_l.append(sp); mkp_l.append(mk_p); mvp_l.append(mv_p)
        ks_l.append(kss); vs_l.append(vss); ss_l.append(sss)
    y_prompt = rms_norm(yp, final_norm_g)
    y_sample = rms_norm(ys, final_norm_g)
    new_diff_k_prompt = jnp.stack(kp_l)
    new_diff_v_prompt = jnp.stack(vp_l)
    new_state_hgrn_prompt = jnp.stack(sp_l)
    new_mem_k_prompt = jnp.stack(mkp_l)
    new_mem_v_prompt = jnp.stack(mvp_l)
    new_diff_k_sample = jnp.stack(ks_l)
    new_diff_v_sample = jnp.stack(vs_l)
    new_state_hgrn_sample = jnp.stack(ss_l)
    return (y_prompt, y_sample, new_diff_k_prompt, new_diff_v_prompt, new_state_hgrn_prompt,
            new_mem_k_prompt, new_mem_v_prompt, new_diff_k_sample, new_diff_v_sample,
            new_state_hgrn_sample)


_drawn_inputs = setup_inputs


def setup_inputs(seed=0):
    import zlib

    import numpy as np

    out = dict(_drawn_inputs(seed))
    spreads = {}
    factors = {'hg_gnorm_g': 3.075,
     'mem_norm_g': 2.848,
     'router_group_b': 10.428,
     'router_expert_b': 4.225,
     'final_norm_g': 8.535,
     'da_subln_g': 4.938,
     'ln_ffn_g': 3.603}
    for name, (base, spread) in spreads.items():
        noise = np.random.default_rng([zlib.crc32(name.encode()), seed]).standard_normal(out[name].shape)
        drawn = base * np.exp(spread * noise) if base else spread * noise
        out[name] = jnp.asarray(drawn.astype(out[name].dtype))
    for name, factor in factors.items():
        out[name] = (out[name] * factor).astype(out[name].dtype)
    return out
```

```python
from contextlib import ExitStack

import concourse.bass as bass
from concourse import mybir

F32 = mybir.dt.float32
I32 = mybir.dt.int32
U32 = mybir.dt.uint32
ALU = mybir.AluOpType
ACT = mybir.ActivationFunctionType
AX_X = mybir.AxisListType.X

P = 128
D = 1024
KC = D // P
SEQ, DEC, PAST, NMEM = 512, 64, 128, 256
TOK = SEQ + DEC
TILES = [(t * P, P) for t in range(SEQ // P)] + [(SEQ, DEC)]
NT = len(TILES)
SAMPLE = NT - 1
H = 4
DA_SCALE = 64 ** -0.5
LAM_INIT = 0.8 - 0.6
SLOPES = [2.0 ** (-2 * (h + 1)) for h in range(H)]
MEM_SCALE = 256 ** -0.5
EPS = 1e-5
BLK = 32
NBLK = TOK // BLK
GROUPS, PER_GROUP = 4, 8
NE = GROUPS * PER_GROUP
FF = 512
CAP = 64
MAX_OVER = (2 * TOK - 1) // CAP
OVER = MAX_OVER + MAX_OVER % 2
NB = NE + OVER
BIG = 1.0e30


class PsumRing:

    def __init__(self, banks, full, free):
        self.banks, self.full, self.free = banks, full, free
        self.filled = self.drained = 0

    def open(self, pe):
        n = len(self.banks)
        if self.filled >= n:
            pe.wait_ge(self.free, self.filled - n + 1)
        return self.banks[self.filled % n]

    def close(self, ins):
        ins.then_inc(self.full, 1)
        self.filled += 1
        return self.filled

    def take(self, eng):
        eng.wait_ge(self.full, self.drained + 1)
        return self.banks[self.drained % len(self.banks)]

    def done(self, ins):
        ins.then_inc(self.free, 1)
        self.drained += 1
        return self.drained


class Chain:

    def __init__(self, eng, sem):
        self.eng, self.sem, self.n = eng, sem, 0

    def step(self, ins):
        ins.then_inc(self.sem, 1)
        self.n += 1

    def settle(self):
        self.eng.wait_ge(self.sem, self.n)

    def link(self, ins):
        self.step(ins)
        self.settle()


def encoder(nc, a, outs):
    (y_prompt, y_sample, nk_p, nv_p, ns_p, nmk, nmv, nk_s, nv_s, ns_s) = outs
    hn_dram = nc.dram_tensor("hn_rows", (TOK, D), F32).ap()
    y_dram = nc.dram_tensor("expert_rows", (NB * CAP, D), F32).ap()

    with ExitStack() as ctx:
        def sem(name):
            return ctx.enter_context(nc.semaphore(name))

        WORDS = 52940
        arena = ctx.enter_context(nc.sbuf_tensor("arena", [P, WORDS], F32))
        ints = ctx.enter_context(nc.sbuf_tensor("ints", [P, 256], I32))
        banks = [ctx.enter_context(nc.psum_tensor(f"bank{i}", [P, 512], F32)) for i in range(6)]
        pair = ctx.enter_context(nc.psum_tensor("score_pair", [P, 2, 512], F32))

        def area(at, *shape, dt=None):
            n = 1
            for s in shape:
                n *= s
            v = arena[:, at:at + n]
            if dt is not None:
                v = v.bitcast(dt)
            if len(shape) == 2:
                v = v.rearrange("p (a b) -> p a b", a=shape[0])
            if len(shape) == 3:
                v = v.rearrange("p (a b c) -> p a b c", a=shape[0], b=shape[1])
            return v

        RING = 0
        NSLOT = 3
        Z1 = RING + NSLOT * 4096
        Z2 = Z1 + 8192
        MZ = Z2 + 9728
        AZ = MZ + 5120
        XZ = AZ + 4608
        OZ = XZ + 5120
        CZ = OZ + 5376

        wslot = [area(RING + 4096 * s, KC, 512) for s in range(NSLOT)]
        qT = area(Z1, H, TOK)
        kT = area(Z1 + 2304, H, TOK)
        ckT = area(Z1 + 4608, H, PAST)
        vN = area(Z1 + 5120, NT, 512)
        cvN = area(Z1 + 7680, 512)
        hqT = area(Z2, H, TOK)
        hfT = area(Z2 + 2304, H, TOK)
        hiN = area(Z2 + 4608, NT, 512)
        hgN = area(Z2 + 7168, NT, 512)
        kN = area(MZ, NT, 512)
        o_da = area(MZ, NT, 512)
        ckN = area(MZ + 2560, 512)
        o_hg = area(MZ + 2560, NT, 512)
        actT = area(AZ, KC, TOK)
        U = [area(XZ + 1024 * i, 2, 512) for i in range(3)]
        wT = [area(XZ + 3072 + 512 * i, 4, P) for i in range(2)]
        stage1 = [area(Z2 + 1024 * i, 1024) for i in range(2)]
        hn1 = [area(Z2 + 2048 + 1024 * i, 1024) for i in range(2)]
        eHG = [area(XZ + 4096 + 512 * i, 512) for i in range(2)]
        gS, gB, gE, gQ = (area(AZ + TOK * i, TOK) for i in range(4))
        kHat = [area(AZ + TOK * (4 + i), TOK) for i in range(2)]
        qHat = [area(AZ + TOK * (6 + i), TOK) for i in range(2)]
        Vbd = area(OZ, NT, 4, P)
        Kt = area(OZ + 2560, NT, P)
        PT = area(OZ + 3200, NT, P)
        Sring = area(OZ + 3840, 12, P)
        stage2 = [area(XZ + 1024 * i, 1024) for i in range(2)]
        hn2 = [area(XZ + 2048 + 1024 * i, 1024) for i in range(2)]
        mkN = area(XZ, 2, 1024)
        mkT = area(Z1, KC, NMEM)
        mvN = area(Z1 + 2048, 2, 1024)
        mnT = area(Z1 + 4096, KC, NMEM)
        cmkT = area(Z1 + 6144, KC, NMEM)
        St0 = area(Z1 + 6144, H, P)
        SF = area(Z1 + 6656, 2 * H, P)
        x_sb = area(XZ, NT, 1024)
        hmT = area(Z2, KC, TOK)
        qmT = area(Z2 + 4608, KC, TOK)
        hn3 = [area(MZ + 1024 * i, 1024) for i in range(2)]
        cmvN = area(MZ + 2048, 2, 1024)
        Pm = [area(MZ + 4096, H, NMEM), area(OZ + 3072, H, NMEM)]
        cmkN = area(OZ, 2, 1024)
        pT = area(OZ + 2048, KC, P)
        E0 = Z1
        wexp = [[area(RING + 4096 * s, KC, 512) for s in range(2)] + [area(RING + 8192, 4, 1024)],
                [area(E0 + 4096 * s, KC, 512) for s in range(2)] + [area(E0 + 8192, 4, 1024)]]
        MB = E0 + 12288
        xg = area(MB, 1024)
        xgT = area(MB + 1024, KC, 2 * CAP)
        eG = area(MB + 2048, 512)
        eU = area(MB + 2560, 512)
        hE = area(MB + 3072, 512)
        hET = area(MB + 3584, 4, 2 * CAP)
        yS = [area(MB + 4096 + 512 * i, 512) for i in range(2)]
        yg = [[area(Z1 + 1024 * (2 * t + k), 1024) for k in range(2)] for t in range(NT)]
        fin = [area(Z1 + 10240 + 1024 * i, 1024) for i in range(2)]
        fjunk = area(Z1 + 12288, 1024)
        gfin = area(AZ, 1024)
        rw = area(AZ + 1024, KC, 36)
        at = [CZ]

        def small(*shape, dt=None):
            n = 1
            for s in shape:
                n *= s
            at[0] += n
            return area(at[0] - n, *shape, dt=dt)

        scanm = small(TOK)
        dist = scanm[:, 0:512]
        ident = small(P)
        ones = small(P)
        upper = small(P)
        bdmask = small(P, dt=I32)
        gains = small(4, KC)
        gsub = small(P)
        ggn = small(P)
        sq = small(512)
        lamp = sq[:, 0:256]
        lamt = sq[:, 256:384].rearrange("p (a b) -> p a b", a=2)
        lam = small(4)
        lbl = small(2, H)
        lb = small(H)
        oml = small(H)
        eps = small(1)
        ssq = small(24)
        rstd = small(24)
        mx = small(2, 4)
        nb = small(2, 4)
        rs = small(2, 4)
        rc = small(2, 4)
        EB = small(H, NBLK)
        hss = small(2 * NT, H)
        hrs = small(2 * NT, H)
        rbias = small(36)
        tokf = small(NT)
        assert at[0] <= WORDS, at[0]
        RZ = [OZ]

        def route(*shape, dt=None):
            n = 1
            for s in shape:
                n *= s
            RZ[0] += n
            return area(RZ[0] - n, *shape, dt=dt)

        lg = route(NT, 36)
        r_g1 = route(NT)
        r_sum = route(NT)
        r_t4 = route(NT, 4)
        r_i4 = route(NT, 4)
        r_e = route(NT, NE)
        r_t = route(NT, NE)
        r_oh = [route(NT, NE) for _ in range(2)]
        r_sel = route(NT, NE)
        r_v = [route(NT) for _ in range(2)]
        r_i = route(NT)
        gate = [route(NT) for _ in range(2)]
        iota32 = route(NE)
        rank_cnt = route((NT + 1) * NE)
        rank = rank_cnt[:, 0:NT * NE].rearrange("p (t e) -> p t e", t=NT)
        cnt = rank_cnt[:, NT * NE:]
        ovf = route(NE)
        cum = route(NE)
        base = route(NE)
        e64 = route(NE)
        ones32 = route(NE)
        r_R = route(NT)
        r_E = route(NT)
        r_O = route(NT)
        slotf = route(2, NT)
        cmp_e = route(OVER, NE)
        eo = route(OVER)
        cmp_p = route(OVER)
        npf = route(1)
        iota_s = route(2 * CAP)
        hot_s = [route(NT, 2 * CAP) for _ in range(2)]
        hot_p = [route(NT, NB // 2) for _ in range(2)]
        lo_f = route(2, NT)
        hi_f = route(2, NT)
        assert RZ[0] <= CZ, RZ[0]
        slot_i = ints[:, 0:2 * NT].rearrange("p (k t) -> p k t", k=2)
        meta_i = ints[:, 16:16 + OVER]
        np_i = ints[:, 40:41]
        sidx = ints[:, 48:48 + NB // 2]
        gidx = ints[:, 100:101]
        gdum = ints[:, 104:108]
        iota_i = ints[:, 108:108 + 2 * CAP]
        tok_i = ints[:, 236:236 + NT]
        lo_i = ints[:, 80:80 + 2 * NT].rearrange("p (k t) -> p k t", k=2)
        hi_i = ints[:, 90:90 + 2 * NT].rearrange("p (k t) -> p k t", k=2)
        dist_i = area(Z2 + 4608, 512, dt=I32)

        ldgain, ldc = sem("first_gain_loaded"), sem("small_loads")
        ldx = [sem(f"x_stage_loaded{i}") for i in range(2)]
        ldw = [sem(f"w_slot_loaded{i}") for i in range(NSLOT)]
        ldcache = sem("caches_loaded")
        ldcm = sem("mem_cache_loaded")
        ldxr = sem("x_reloaded")
        ldrt = sem("router_loaded")
        pool_c = sem("pool_constants")
        pool_s = sem("pool_steps")
        cst = sem("vector_constants")
        dv = sem("vector_chain")
        ac = sem("scalar_chain")
        c_in, c_exp = sem("constant_exp_input"), sem("constant_exp")
        a_full, a_free = sem("a_bank_full"), sem("a_bank_drained")
        v_full, v_free = sem("v_bank_full"), sem("v_bank_drained")
        s_full, s_free = sem("score_pair_full"), sem("score_pair_read")
        ssq_ready, rstd_ready, hn_ready = sem("ssq_ready"), sem("rstd_ready"), sem("hn_ready")
        nb_ready, p_ready, w_ready = sem("neg_max_ready"), sem("probs_ready"), sem("diff_weights_ready")
        hss_ready, hrs_ready, mix_ready = sem("head_ssq_ready"), sem("head_rstd_ready"), sem("mixed_ready")
        pre_act, pre_dve = sem("hgrn_pre_scalar"), sem("hgrn_pre_vector")
        vbd_ready = sem("v_blocks_ready")
        eg_ready, sg_ready = sem("exp_gate_ready"), sem("swish_gate_ready")
        mnb_ready, mp_ready, mpn_ready = sem("mem_neg_max"), sem("mem_probs"), sem("mem_probs_scaled")
        hn_st = [sem(f"hn_rows_stored{i}") for i in range(2)]
        stk, stv, sts, stmk, stmv = (sem(f"stored_{n}") for n in ("k", "v", "state", "mem_k", "mem_v"))
        r_exp = sem("router_exp")
        r_need = sem("router_exp_input")
        sel_ready, slot_ready, meta_ready = sem("selection_ready"), sem("slots_ready"), sem("meta_ready")
        y_zero = sem("spare_rows_zeroed")
        hot_ready = sem("slot_one_hots_ready")
        ldg = [sem(f"w_gate_loaded{j}") for j in range(2)]
        ldu = [sem(f"w_up_loaded{j}") for j in range(2)]
        ldd = [sem(f"w_down_loaded{j}") for j in range(2)]
        xg_ld = sem("rows_gathered")
        gi_ready = sem("gather_index_ready")
        tx_full, gu_full, th_full, dn_full = (sem(n) for n in ("xT_in_psum", "gate_up_done", "hT_in_psum", "down_done"))
        xT_cp, hE_ready, hT_cp, y_cp = (sem(n) for n in ("xT_copied", "h_ready", "hT_copied", "y_copied"))
        act_u, mdv = sem("exp_and_up_copied"), sem("moe_vector_chain")
        y_st = [sem(f"y_rows_stored{j}") for j in range(2)]
        y_all = sem("all_y_stored")
        yg_ld = [sem(f"y_rows_gathered{t}") for t in range(NT)]
        fssq, frstd, fin_ready, fin_st = sem("final_ssq"), sem("final_rstd"), sem("final_ready"), [sem(f"final_stored{i}") for i in range(2)]

        A = PsumRing(banks[0:3], a_full, a_free)
        V = PsumRing(banks[3:6], v_full, v_free)
        mark = {}

        UNITS = [("w_in", 512 * c) for c in (0, 1, 2, 4, 3, 5, 6)]
        UNITS += [("w_mem_k", 0), ("w_mem_k", 512), ("w_mem_v", 0), ("w_mem_v", 512)]
        UNITS += [("w_out", 0), ("w_out", 512), ("w_mem_q", 0), ("w_mem_q", 512), ("w_mem_o", 0), ("w_mem_o", 512)]
        unit_done = {}
        NCONST = 9

        block = ctx.enter_context(nc.Block())

        def moe_loops(eng, body):
            body(0)
            with eng.Fori(1, NE // 2) as i:
                body(i)
            eng.wait_ge(meta_ready, 1)
            pairs = eng.value_load(np_i[0:1, 0:1], min_val=0, max_val=OVER // 2)
            with eng.If(pairs > 0):
                with eng.Fori(NE // 2, pairs + NE // 2) as i:
                    body(i)
            return pairs

        @block.tensor
        def _(pe):
            mm, tr = nc.tensor.matmul, nc.tensor.transpose
            pe.wait_ge(pool_c, 1)

            def norm(n, hn, rows):
                pe.wait_ge(hn_ready, n + 1)
                for half in range(2):
                    b = V.open(pe)
                    for c in range(4):
                        k = 4 * half + c
                        ins = tr(b[:, c * P:c * P + rows], hn[0:rows, k * P:(k + 1) * P], ident[0:rows, 0:rows])
                    mark["norm", n, half] = V.close(ins)

            def weights(u):
                pe.wait_ge(ldw[u % NSLOT], 16 * (u // NSLOT + 1))
                return wslot[u % NSLOT]

            def proj_T(u, src, c):
                w = weights(u)
                b = A.open(pe)
                if c < 4:
                    for k in range(KC):
                        ins = mm(b[:, 0:SEQ], w[:, k, c * P:(c + 1) * P], src[:, k, 0:SEQ], start=k == 0, stop=k == KC - 1)
                else:
                    for cc in range(4):
                        for k in range(KC):
                            ins = mm(b[:, cc * DEC:(cc + 1) * DEC], w[:, k, cc * P:(cc + 1) * P], src[:, k, SEQ:TOK],
                                     start=k == 0, stop=k == KC - 1)
                unit_done[u] = (a_full, A.close(ins))
                mark["proj", u, c] = A.filled

            def proj_N(u, src, t, ring, tiles=TILES):
                w = weights(u)
                t0, rows = tiles[t]
                b = ring.open(pe)
                for k in range(KC):
                    ins = mm(b[0:rows, :], src[:, k, t0:t0 + rows], w[:, k, :], start=k == 0, stop=k == KC - 1)
                unit_done[u] = (ring.full, ring.close(ins))
                mark["proj", u, t] = ring.filled

            for n, (_, rows) in enumerate(TILES):
                norm(n, hn1[n % 2], rows)
            pe.wait_ge(v_free, mark["norm", SAMPLE, 1])
            for c in range(5):
                proj_T(0, actT, c)
            for t in range(NT):
                proj_N(1, actT, t, A)
            for t in range(NT):
                rows = TILES[t][1]
                b = A.open(pe)
                pe.wait_ge(a_free, mark["proj", 1, t])
                for h in range(H):
                    ins = tr(b[:, h * P:h * P + rows], kN[0:rows, t, h * P:(h + 1) * P], ident[0:rows, 0:rows])
                mark["kT", t] = A.close(ins)
            b = A.open(pe)
            pe.wait_ge(ldcache, 32)
            for h in range(H):
                ins = tr(b[:, h * P:(h + 1) * P], ckN[:, h * P:(h + 1) * P], ident)
            mark["ckT"] = A.close(ins)
            for t in range(NT):
                proj_N(2, actT, t, A)

            def scores(i):
                t, h = divmod(i, H)
                t0, rows = TILES[t]
                if i == 0:
                    pe.wait_ge(a_free, mark["ckT"])
                if i >= 1:
                    pe.wait_ge(s_free, i)
                for c in range(2):
                    lo = 64 * c
                    q = qT[lo:lo + 64, h, t0:t0 + rows]
                    if t < SAMPLE:
                        ins = mm(pair[0:rows, c, 0:t0 + P], q, kT[lo:lo + 64, h, 0:t0 + P], start=True, stop=True)
                    else:
                        mm(pair[0:rows, c, 0:PAST], q, ckT[lo:lo + 64, h, :], start=True, stop=True)
                        ins = mm(pair[0:rows, c, PAST:PAST + DEC], q, kT[lo:lo + 64, h, SEQ:TOK], start=True, stop=True)
                ins.then_inc(s_full, 1)

            def key_blocks(t):
                if t < SAMPLE:
                    return [(P * j, P) for j in range(t + 1)]
                return [(0, PAST), (PAST, DEC)]

            def turn_weights(i):
                t, h = divmod(i, H)
                rows = TILES[t][1]
                pe.wait_ge(w_ready, i + 1)
                b = A.open(pe)
                for j, (k0, n) in enumerate(key_blocks(t)):
                    ins = tr(b[0:n, j * P:j * P + rows], U[i % 3][0:rows, 0, k0:k0 + n], ident[0:rows, 0:rows])
                mark["wT", i] = A.close(ins)

            def weigh_values(i):
                t, h = divmod(i, H)
                rows = TILES[t][1]
                pe.wait_ge(a_free, mark["wT", i])
                if i == 0:
                    pe.wait_ge(a_free, mark["proj", 2, SAMPLE])
                b = V.open(pe)
                kb = key_blocks(t)
                for j, (k0, n) in enumerate(kb):
                    if t < SAMPLE:
                        v = vN[:, j, h * P:(h + 1) * P]
                    else:
                        v = cvN[:, h * P:(h + 1) * P] if j == 0 else vN[0:n, SAMPLE, h * P:(h + 1) * P]
                    ins = mm(b[0:rows, 0:P], wT[i % 2][0:n, j, 0:rows], v, start=j == 0, stop=j == len(kb) - 1)
                mark["o_da", t] = V.close(ins)

            for i in range(NT * H + 2):
                if i < NT * H:
                    scores(i)
                if 1 <= i <= NT * H:
                    turn_weights(i - 1)
                if i >= 2:
                    weigh_values(i - 2)
                if i < 10:
                    proj_T(3 + i // 5, actT, i % 5)
                elif i < 20:
                    proj_N(3 + i // 5, actT, i % 5, A)

            MT = [(0, P), (P, P)]
            for m in range(2):
                norm(NT + m, hn2[m], P)
            pe.wait_ge(v_free, mark["norm", NT + 1, 1])

            def mem_kv(j):
                proj_N(7 + j // 2, mnT, j % 2, A, MT)

            def hgrn(h):
                pe.wait_ge(pre_dve, 3 * h + 3)
                b = V.open(pe)
                for t in range(4):
                    s = slice(t * P, (t + 1) * P)
                    ins = mm(b[:, t * P:(t + 1) * P], kHat[h % 2][:, s], qHat[h % 2][:, s], start=True, stop=True)
                V.close(ins)
                b = V.open(pe)
                ins = mm(b[0:DEC, 0:DEC], kHat[h % 2][:, SEQ:TOK], qHat[h % 2][:, SEQ:TOK], start=True, stop=True)
                mark["PT", h] = V.close(ins)
                b = A.open(pe)
                for t in range(4):
                    ins = tr(b[:, t * P:(t + 1) * P], hfT[:, h, t * P:(t + 1) * P], ident)
                A.close(ins)
                b = A.open(pe)
                mark["Kt", h] = A.close(tr(b[0:DEC, 0:P], hfT[:, h, SEQ:TOK], ident))
                state_at = {}

                def increments(t):
                    rows = TILES[t][1]
                    nb4 = rows // BLK
                    if t == 0:
                        pe.wait_ge(vbd_ready, h + 1)
                        pe.wait_ge(a_free, mark["Kt", h])
                    b = V.open(pe)
                    ins = mm(b[:, 0:nb4 * P].rearrange("p (j v) -> p j v", j=nb4), Kt[0:rows, t, :],
                             Vbd[0:rows, t, 0:nb4, :], start=True, stop=True)
                    state_at[t] = V.close(ins)
                    mark["G", h, t] = V.filled

                def outputs(t):
                    t0, rows = TILES[t]
                    pe.wait_ge(v_free, mark["PT", h])
                    pe.wait_ge(v_free, state_at[t])
                    if t == SAMPLE:
                        pe.wait_ge(ldcache, 48)
                    b = V.open(pe)
                    ins = mm(b[0:rows, 0:P], PT[0:rows, t, 0:rows], hiN[0:rows, t, h * P:(h + 1) * P],
                             start=True, stop=False, skip_group_check=True)
                    for j in range(rows // BLK):
                        g = 4 * t + j
                        if g == 0:
                            continue
                        s0 = St0[:, h, :] if t == SAMPLE and j == 0 else Sring[:, (h * NBLK + g) % 12, :]
                        ins = mm(b[BLK * j:BLK * (j + 1), 0:P], hqT[:, h, t0 + BLK * j:t0 + BLK * (j + 1)], s0,
                                 start=False, stop=True, skip_group_check=True)
                    mark["O", h, t] = V.close(ins)

                increments(0)
                for t in range(NT):
                    if t + 1 < NT:
                        increments(t + 1)
                    outputs(t)

            for h in range(H):
                mem_kv(2 * h)
                mem_kv(2 * h + 1)
                hgrn(h)
            for half in range(2):
                for m in range(2):
                    b = A.open(pe)
                    pe.wait_ge(a_free, mark["proj", 8, 1])
                    for c in range(4):
                        k = 4 * half + c
                        ins = tr(b[:, c * P:(c + 1) * P], mkN[:, m, k * P:(k + 1) * P], ident)
                    mark["mkT"] = A.close(ins)
            for part, src in enumerate((o_da, o_hg)):
                for t, (t0, rows) in enumerate(TILES):
                    pe.wait_ge(mix_ready, part * NT + t + 1)
                    b = A.open(pe)
                    for c in range(4):
                        ins = tr(b[:, c * P:c * P + rows], src[0:rows, t, c * P:(c + 1) * P], ident[0:rows, 0:rows])
                    mark["mixT"] = A.close(ins)
            for t in range(NT):
                if t == 0:
                    pe.wait_ge(a_free, mark["mixT"])
                for n in range(2):
                    proj_N(11 + n, actT, t, V)
                    mark["x1", t] = V.filled
                if t >= 1:
                    norm(7 + t - 1, hn3[(t - 1) % 2], TILES[t - 1][1])
            norm(7 + SAMPLE, hn3[SAMPLE % 2], DEC)
            for half in range(2):
                for m in range(2):
                    b = A.open(pe)
                    pe.wait_ge(ldcm, 32)
                    for c in range(4):
                        k = 4 * half + c
                        ins = tr(b[:, c * P:(c + 1) * P], cmkN[:, m, k * P:(k + 1) * P], ident)
                    A.close(ins)
            pe.wait_ge(v_free, mark["norm", 7 + SAMPLE, 1])
            for u in (13, 14):
                for c in range(5):
                    proj_T(u, hmT, c)

            def mem_scores(t):
                t0, rows = TILES[t]
                if t == 0:
                    pe.wait_ge(a_free, mark["proj", 14, 4])
                    pe.wait_ge(s_free, NT * H)
                else:
                    pe.wait_ge(mp_ready, t)
                keys = mkT if t < SAMPLE else cmkT
                for h in range(H):
                    for c in range(2):
                        o = pair[0:rows, h // 2, (h % 2) * NMEM:(h % 2 + 1) * NMEM]
                        ins = mm(o, qmT[:, 2 * h + c, t0:t0 + rows], keys[:, 2 * h + c, :], start=c == 0, stop=c == 1)
                ins.then_inc(s_full, 1)

            def mem_values(t):
                t0, rows = TILES[t]
                pe.wait_ge(mpn_ready, t + 1)
                for half in range(2):
                    b = A.open(pe)
                    for c in range(4):
                        j = 4 * half + c
                        ins = tr(b[:, c * P:c * P + rows], Pm[t % 2][0:rows, j // 2, (j % 2) * P:(j % 2 + 1) * P],
                                 ident[0:rows, 0:rows])
                    done = A.close(ins)
                pe.wait_ge(a_free, done)
                if t == SAMPLE:
                    pe.wait_ge(ldcm, 32)
                vals = mvN if t < SAMPLE else cmvN
                for half in range(2):
                    b = V.open(pe)
                    for c in range(4):
                        j = 4 * half + c
                        for m in range(2):
                            ins = mm(b[:, c * P:c * P + rows], vals[:, m, j * P:(j + 1) * P],
                                     pT[:, 2 * (j // 2) + m, 0:rows], start=m == 0, stop=m == 1)
                    mark["omT"] = V.close(ins)

            for t in range(NT + 1):
                if t < NT:
                    mem_scores(t)
                if t >= 1:
                    mem_values(t - 1)
            pe.wait_ge(v_free, mark["omT"])
            for t in range(NT):
                for n in range(2):
                    proj_N(15 + n, actT, t, V)
                    mark["x2", t] = V.filled
                if t >= 1:
                    norm(12 + t - 1, hn3[(t - 1) % 2], TILES[t - 1][1])
            norm(12 + SAMPLE, hn3[SAMPLE % 2], DEC)
            pe.wait_ge(ldrt, 48)
            for t, (t0, rows) in enumerate(TILES):
                pe.wait_ge(v_free, mark["norm", 12 + t, 1])
                b = V.open(pe)
                for k in range(KC):
                    ins = mm(b[0:rows, 0:36], hmT[:, k, t0:t0 + rows], rw[:, k, :], start=k == 0, stop=k == KC - 1)
                V.close(ins)
            pe.wait_ge(sel_ready, 1)
            b = V.open(pe)
            for t in range(NT + 1):
                last = min(t, NT - 1)
                for j in range(last + 1):
                    w = upper if j == t else ones
                    ins = mm(b[:, t * NE:(t + 1) * NE], w, r_sel[:, j, :], start=j == 0, stop=j == last)
            V.close(ins)
            pe.wait_ge(hot_ready, 1)
            b = V.open(pe)
            for k in range(2):
                for t, (_, rows) in enumerate(TILES):
                    ins = mm(b[:, 0:NB // 2], hot_s[k][0:rows, t, :], hot_p[k][0:rows, t, :], start=k == 0 and t == 0,
                             stop=k == 1 and t == SAMPLE)
            mark["sidx"] = V.close(ins)
            pe.wait_ge(v_free, V.filled)
            pe.wait_ge(a_free, A.filled)

            def pair_of_blocks(i):
                later = not isinstance(i, int)
                pe.wait_ge(xg_ld, 16 * (i + 1))
                for k in range(KC):
                    ins = tr(pair[:, k // 4, (k % 4) * P:(k % 4 + 1) * P], xg[:, k * P:(k + 1) * P], ident)
                ins.then_inc(tx_full, 1)
                for j in range(2):
                    pe.wait_ge(ldg[j], 16 * (i + 1))
                    pe.wait_ge(ldu[j], 16 * (i + 1))
                    if j == 0:
                        pe.wait_ge(xT_cp, i + 1)
                    g, u = banks[1 + j][CAP * j:CAP * (j + 1), :], banks[1 + j][CAP * (1 - j):CAP * (2 - j), :]
                    for k in range(KC):
                        x = xgT[:, k, CAP * j:CAP * (j + 1)]
                        mm(g, x, wexp[j][0][:, k, :], start=k == 0, stop=k == KC - 1)
                        ins = mm(u, x, wexp[j][1][:, k, :], start=k == 0, stop=k == KC - 1)
                    ins.then_inc(gu_full, 1)
                pe.wait_ge(hE_ready, i + 1)
                for k in range(4):
                    ins = tr(banks[3][:, k * P:(k + 1) * P], hE[:, k * P:(k + 1) * P], ident)
                ins.then_inc(th_full, 1)
                pe.wait_ge(hT_cp, i + 1)
                if later:
                    pe.wait_ge(y_cp, 2 * i)
                for j in range(2):
                    pe.wait_ge(ldd[j], 16 * (i + 1))
                    for k in range(4):
                        for n in range(2):
                            ins = mm(banks[4 + j][CAP * n:CAP * (n + 1), :], hET[:, k, CAP * j:CAP * (j + 1)],
                                     wexp[j][2][:, k, 512 * n:512 * (n + 1)], start=k == 0, stop=k == 3)
                    ins.then_inc(dn_full, 1)

            moe_loops(pe, pair_of_blocks)

        @block.sync
        def _(sp):
            def load_unit(u):
                if u >= NSLOT:
                    s, n = unit_done[u - NSLOT]
                    sp.wait_ge(s, n)
                name, c = UNITS[u]
                src = a[name][0].rearrange("(k p) n -> p k n", p=P)[:, :, c:c + 512]
                sp.dma_start(wslot[u % NSLOT], src).then_inc(ldw[u % NSLOT], 16)

            def rows_of_x(t):
                t0, rows = TILES[t]
                return a["x_prompt"][0, t0:t0 + rows, :] if t < SAMPLE else a["x_sample"][0]

            def load_stage(n, dst, src, rows):
                sp.dma_start(dst[0:rows, :], src).then_inc(ldx[n % 2], 16)

            load_stage(0, stage1[0], rows_of_x(0), P)
            load_stage(1, stage1[1], rows_of_x(1), P)
            load_unit(0)
            for n in (2, 3, 4):
                sp.wait_ge(hn_ready, n - 1)
                load_stage(n, stage1[n % 2], rows_of_x(n), TILES[n][1])
            load_unit(1)
            load_unit(2)
            sp.wait_ge(pool_c, 1)
            sp.dma_start(y_dram[NE * CAP:, :].rearrange("(c p) n -> p c n", p=P),
                         area(OZ, 1024).unsqueeze(1).broadcast_to([P, OVER * CAP // P, 1024])).then_inc(y_zero, 16)
            sp.dma_start(ckN, a["cache_diff_k"][0, 0].rearrange("t h d -> t (h d)")).then_inc(ldcache, 16)
            sp.dma_start(cvN, a["cache_diff_v"][0, 0].rearrange("t h d -> t (h d)")).then_inc(ldcache, 16)
            load_unit(3)
            load_unit(4)
            sp.wait_ge(a_free, mark["proj", 1, SAMPLE])
            sp.dma_start(nk_p[0, 0].rearrange("(t p) h d -> p t (h d)", p=P), kN[:, 0:4, :]).then_inc(stk, 16)
            sp.dma_start(nk_s[0, 0].rearrange("t h d -> t (h d)"), kN[0:DEC, SAMPLE, :]).then_inc(stk, 16)
            sp.wait_ge(a_free, mark["proj", 2, SAMPLE])
            sp.dma_start(nv_p[0, 0].rearrange("(t p) h d -> p t (h d)", p=P), vN[:, 0:4, :]).then_inc(stv, 16)
            sp.dma_start(nv_s[0, 0].rearrange("t h d -> t (h d)"), vN[0:DEC, SAMPLE, :]).then_inc(stv, 16)
            load_unit(5)
            load_unit(6)
            sp.wait_ge(w_ready, NT * H)
            sp.wait_ge(a_free, mark["wT", NT * H - 1])
            sp.wait_ge(v_free, mark["o_da", SAMPLE])
            sp.wait_ge(ldcache, 32)
            sp.dma_start(St0, a["state_hgrn"][0, 0].rearrange("h d v -> d h v")).then_inc(ldcache, 16)
            for m in range(2):
                load_stage(5 + m, stage2[m], a["mem_prompt"][0, m * P:(m + 1) * P, :], P)
            for u in range(7, 11):
                load_unit(u)
            sp.wait_ge(a_free, mark["proj", 8, 1])
            sp.dma_start(nmk[0, 0].rearrange("(m p) h d -> p m (h d)", p=P), mkN).then_inc(stmk, 16)
            sp.wait_ge(a_free, mark["proj", 10, 1])
            sp.dma_start(nmv[0, 0].rearrange("(m p) h d -> p m (h d)", p=P), mvN).then_inc(stmv, 16)
            load_unit(11)
            load_unit(12)
            sp.wait_ge(a_free, mark["mkT"])
            sp.wait_ge(stmk, 16)
            sp.wait_ge(sg_ready, NT)
            sp.dma_start(x_sb[:, 0:4, :], a["x_prompt"][0].rearrange("(t p) n -> p t n", p=P)).then_inc(ldxr, 16)
            sp.dma_start(x_sb[0:DEC, SAMPLE, :], a["x_sample"][0]).then_inc(ldxr, 16)
            sp.wait_ge(v_free, mark["G", H - 1, SAMPLE])
            sp.dma_start(ns_p[0, 0].rearrange("h d v -> d h v"), SF[:, 0:H, :]).then_inc(sts, 16)
            sp.dma_start(ns_s[0, 0].rearrange("h d v -> d h v"), SF[:, H:2 * H, :]).then_inc(sts, 16)
            load_unit(13)
            sp.wait_ge(a_free, mark["mixT"])
            sp.dma_start(cmkN, a["cache_mem_k"][0, 0].rearrange("(m p) h d -> p m (h d)", p=P)).then_inc(ldcm, 16)
            sp.dma_start(cmvN, a["cache_mem_v"][0, 0].rearrange("(m p) h d -> p m (h d)", p=P)).then_inc(ldcm, 16)
            for u in (14, 15, 16):
                load_unit(u)

            def load_part(j, which, e):
                name = ("exp_w_gate", "exp_w_up", "exp_w_down")[which]
                src = a[name][0, e:e + 1] if isinstance(e, int) else a[name][0][bass.ds(e, 1)]
                sp.dma_start(wexp[j][which], src.rearrange("o (k p) n -> p (o k) n", p=P)).then_inc((ldg, ldu, ldd)[which][j], 16)

            sp.wait_ge(v_free, mark["omT"])
            load_part(1, 0, 1)
            load_part(1, 1, 1)
            for n in range(NT):
                sp.wait_ge(hn_ready, 12 + n + 1)
                t0, rows = TILES[n]
                sp.dma_start(hn_dram[t0:t0 + rows, :], hn3[n % 2][0:rows, :]).then_inc(hn_st[n % 2], 16)
                if n == NT - 1:
                    s, v = unit_done[16]
                    sp.wait_ge(s, v)
                    sp.dma_start(rw[:, :, 0:4], a["router_group_w"][0].rearrange("(k p) n -> p k n", p=P)).then_inc(ldrt, 16)
                    sp.dma_start(rw[:, :, 4:36], a["router_expert_w"][0].rearrange("(k p) n -> p k n", p=P)).then_inc(ldrt, 16)
                    sp.dma_start(gfin, a["final_norm_g"].rearrange("(o n) -> o n", o=1).broadcast_to([P, D])).then_inc(ldrt, 16)
            for which in range(3):
                load_part(0, which, 0)
            sp.wait_ge(v_free, mark["norm", 12 + SAMPLE, 1])
            sp.wait_ge(sel_ready, 1)
            load_part(1, 2, 1)

            def load_pair(i, e):
                for j in range(2):
                    sp.wait_ge(gu_full, 2 * i + (j - 1))
                    load_part(j, 0, e[j])
                    load_part(j, 1, e[j])
                for j in range(2):
                    sp.wait_ge(dn_full, 2 * i + (j - 1))
                    load_part(j, 2, e[j])

            with sp.Fori(1, NE // 2) as i:
                load_pair(i, [2 * i, 2 * i + 1])
            sp.wait_ge(meta_ready, 1)
            pairs = sp.value_load(np_i[0:1, 0:1], min_val=0, max_val=OVER // 2)
            with sp.If(pairs > 0):
                with sp.Fori(NE // 2, pairs + NE // 2) as i:
                    load_pair(i, [sp.value_load(meta_i[0:1, bass.ds(2 * i + (j - NE), 1)], min_val=0, max_val=NE - 1)
                                  for j in range(2)])
            for t, (t0, rows) in enumerate(TILES):
                sp.wait_ge(fin_ready, t + 1)
                dst = y_prompt[0, t0:t0 + rows, :] if t < SAMPLE else y_sample[0]
                sp.dma_start(dst, fin[t % 2][0:rows, :]).then_inc(fin_st[t % 2], 16)
            for s, n in ((stk, 32), (stv, 32), (sts, 32), (stmk, 16), (stmv, 16), (hn_st[0], 48), (hn_st[1], 32),
                         (fin_st[0], 48), (fin_st[1], 32)):
                sp.wait_ge(s, n)

        @block.gpsimd
        def _(po):
            g = nc.gpsimd
            n = Chain(po, pool_s)
            n.step(g.memset(ident, 0.0))
            n.step(g.memset(ones, 1.0))
            n.step(g.memset(upper, 1.0))
            n.step(g.memset(bdmask, 1))
            n.step(g.iota(dist_i, pattern=[[-1, 512]], base=SEQ - P, channel_multiplier=1))
            n.settle()
            n.step(g.affine_select(out=upper, in_=upper, pattern=[[1, P]], compare_op=ALU.is_gt, fill=0.0, base=0, channel_multiplier=-1))
            n.step(g.affine_select(out=bdmask, in_=bdmask, pattern=[[1, P]], compare_op=ALU.is_ge, fill=0, base=0, channel_multiplier=-1))
            n.settle()
            bd3 = bdmask.rearrange("p (j c) -> p j c", j=4)
            n.step(g.affine_select(out=bd3, in_=bd3, pattern=[[-BLK, 4], [0, BLK]], compare_op=ALU.is_ge, fill=0, base=0, channel_multiplier=1))
            n.step(g.iota(iota_i, pattern=[[1, 2 * CAP]], base=0, channel_multiplier=0))
            n.step(g.iota(tok_i, pattern=[[P, NT]], base=0, channel_multiplier=1))
            n.step(g.memset(eps, EPS))
            n.step(g.memset(PT, 0.0))
            n.step(g.memset(Vbd, 0.0))
            n.settle()
            g.affine_select(out=ident, in_=ident, pattern=[[-1, P]], compare_op=ALU.not_equal, fill=1.0, base=0,
                            channel_multiplier=1).then_inc(pool_c, 1)

            def head_norm(k, src, t, gain):
                rows = TILES[t][1]
                v = src[0:rows, t, :]
                v3 = v.rearrange("p (h d) -> p h d", h=H)
                n.link(g.tensor_tensor(sq[0:rows, :], v, v, ALU.mult))
                w = P // 2
                while w > 1:
                    q = sq[0:rows, :].rearrange("p (h d) -> p h d", h=H)
                    n.link(g.tensor_tensor(q[:, :, 0:w], q[:, :, 0:w], q[:, :, w:2 * w], ALU.add))
                    w //= 2
                g.tensor_tensor(hss[0:rows, k, :].unsqueeze(2), q[:, :, 0:1], q[:, :, 1:2], ALU.add).then_inc(hss_ready, 1)
                po.wait_ge(hrs_ready, k + 1)
                n.link(g.tensor_tensor(v3, v3, hrs[0:rows, k, :].unsqueeze(2).broadcast_to([rows, H, P]), ALU.mult))
                g.tensor_tensor(v3, v3, gain, ALU.mult).then_inc(mix_ready, 1)
                po.wait_ge(mix_ready, k + 1)

            po.wait_ge(cst, 1)
            for t in range(NT):
                po.wait_ge(v_free, mark["o_da", t])
                rows = TILES[t][1]
                head_norm(t, o_da, t, gsub[0:rows, :].unsqueeze(1).broadcast_to([rows, H, P]))
            for h in range(H):
                if h == 0:
                    po.wait_ge(y_zero, 16)
                    po.wait_ge(a_free, mark["proj", 5, SAMPLE])
                else:
                    po.wait_ge(vbd_ready, h)
                    po.wait_ge(v_full, mark["G", h - 1, SAMPLE])
                for j in range(4):
                    nt = NT if j < DEC // BLK else NT - 1
                    s = slice(BLK * j, BLK * (j + 1))
                    ins = g.tensor_copy(Vbd[s, 0:nt, j, :], hiN[s, 0:nt, h * P:(h + 1) * P])
                    if j < 3:
                        n.link(ins)
                ins.then_inc(vbd_ready, 1)
            for t in range(NT):
                rows = TILES[t][1]
                po.wait_ge(v_free, mark["O", H - 1, t])
                po.wait_ge(sg_ready, t + 1)
                head_norm(NT + t, o_hg, t, hgN[0:rows, t, :].rearrange("p (h d) -> p h d", h=H))
            po.wait_ge(slot_ready, 1)
            po.wait_ge(v_free, mark["sidx"])
            po.wait_ge(hn_st[0], 48)
            po.wait_ge(hn_st[1], 32)
            n.link(g.memset(gdum, 0))

            def pair_of_blocks(i):
                if not isinstance(i, int):
                    po.wait_ge(tx_full, i)
                g.tensor_copy(gidx, sidx[:, bass.ds(i, 1)]).then_inc(gi_ready, 1)
                po.wait_ge(gi_ready, i + 1)
                g.tensor_tensor(gdum[:, 0:1], gdum[:, 1:2], gdum[:, 2:3], ALU.add)
                g.indirect_dma_start(out=xg, out_offset=None, in_=hn_dram,
                                     in_offset=bass.IndirectOffsetOnAxis(ap=gidx, axis=0)).then_inc(xg_ld, 16)

            moe_loops(po, pair_of_blocks)
            po.wait_ge(y_all, 1)
            for t, (_, rows) in enumerate(TILES):
                for k in range(2):
                    g.indirect_dma_start(out=yg[t][k][0:rows, :], out_offset=None, in_=y_dram,
                                         in_offset=bass.IndirectOffsetOnAxis(ap=slot_i[0:rows, k, t:t + 1], axis=0)).then_inc(yg_ld[t], 16)

        @block.scalar
        def _(act):
            f = nc.scalar.activation
            n = Chain(act, ac)

            def row(ap, width, parts=P):
                return ap.rearrange("(o n) -> o n", o=1).broadcast_to([parts, width])

            for i, name in enumerate(("ln_mix_g", "mem_norm_g", "ln_mem_g", "ln_ffn_g")):
                act.dma_start(gains[:, i, :], a[name][0].rearrange("(k p) -> p k", p=P),
                              allow_slow_non_contiguous=True).then_inc(ldc if i else ldgain, 16)
            act.dma_start(gsub, row(a["da_subln_g"][0], P)).then_inc(ldc, 16)
            act.dma_start(ggn, row(a["hg_gnorm_g"][0], P)).then_inc(ldc, 16)
            act.dma_start(lamp, row(a["da_lambda"][0].rearrange("f d -> (f d)"), 256)).then_inc(ldc, 16)
            act.dma_start(lbl, a["hg_lb_logits"].rearrange("l (h p) -> p l h", p=P),
                          allow_slow_non_contiguous=True).then_inc(ldc, 16)
            act.dma_start(rbias[:, 0:GROUPS], row(a["router_group_b"][0], GROUPS)).then_inc(ldc, 16)
            act.dma_start(rbias[:, GROUPS:], row(a["router_expert_b"][0], NE)).then_inc(ldc, 16)
            act.wait_ge(pool_c, 1)

            def inv_std(out, total, count, ready):
                rows = out.shape[0]
                n.link(f(out, total, ACT.Ln, bias=eps[0:rows, :], scale=1.0 / count))
                f(out, out, ACT.Exp, scale=-0.5).then_inc(ready, 1)

            def norm(p, rows):
                act.wait_ge(ssq_ready, p + 1)
                inv_std(rstd[0:rows, p:p + 1], ssq[0:rows, p:p + 1], D, rstd_ready)

            def drain(dst, get):
                b = A.take(act)
                A.done(f(dst, get(b), ACT.Copy))

            def quads(rows):
                return lambda b: b[:, :].rearrange("p (c t) -> p c t", c=4)[:, :, 0:rows]

            def drain_T(dst):
                for c in range(5):
                    drain_T1(dst, c)

            def drain_T1(dst, c):
                if c < 4:
                    drain(dst[:, c, 0:SEQ], lambda b: b[:, :])
                else:
                    drain(dst[:, :, SEQ:TOK], lambda b: b[:, 0:4 * DEC].rearrange("p (c t) -> p c t", c=4))

            def drain_N(dst, t):
                rows = TILES[t][1]
                drain(dst[0:rows, t, :], lambda b: b[0:rows, :])

            for p, (_, rows) in enumerate(TILES):
                norm(p, rows)
            act.wait_ge(c_in, 1)
            f(lbl, lbl, ACT.Exp).then_inc(c_exp, 1)
            f(lam[:, 0:2], lam[:, 0:2], ACT.Exp).then_inc(c_exp, 1)
            drain_T(qT)
            for t in range(NT):
                drain_N(kN, t)
            for t, (t0, rows) in enumerate(TILES):
                drain(kT[:, :, t0:t0 + rows], quads(rows))
            drain(ckT, quads(P))
            for t in range(NT):
                drain_N(vN, t)

            def head_rstd(k, rows):
                act.wait_ge(hss_ready, k + 1)
                inv_std(hrs[0:rows, k, :], hss[0:rows, k, :], P, hrs_ready)

            def exps(i):
                t, h = divmod(i, H)
                rows = TILES[t][1]
                keys = (t + 1) * P if t < SAMPLE else PAST + DEC
                act.wait_ge(nb_ready, i + 1)
                for c in range(2):
                    u = U[i % 3][0:rows, c, 0:keys]
                    ins = f(u, u, ACT.Exp, bias=nb[0:rows, i % 2, c:c + 1], scale=DA_SCALE,
                            accum_out=rs[0:rows, i % 2, c:c + 1])
                ins.then_inc(p_ready, 1)

            for i in range(NT * H + 1):
                if i < NT * H:
                    exps(i)
                if i >= 1:
                    t = (i - 1) // H
                    rows = TILES[t][1]
                    blocks = t + 1 if t < SAMPLE else 1
                    if t < SAMPLE:
                        drain(wT[(i - 1) % 2][:, 0:blocks, :], lambda b: b[:, 0:blocks * P].rearrange("p (j q) -> p j q", q=P))
                    else:
                        b = A.take(act)
                        n.step(f(wT[(i - 1) % 2][:, 0, 0:rows], b[:, 0:rows], ACT.Copy))
                        A.done(f(wT[(i - 1) % 2][0:DEC, 1, 0:rows], b[0:DEC, P:P + rows], ACT.Copy))
                if i < 5:
                    drain_T1(hfT, i)
                elif i < 10:
                    drain_T1(hqT, i - 5)
                elif i < 15:
                    drain_N(hiN, i - 10)
                elif i < 20:
                    drain_N(hgN, i - 15)
                if i >= 7 and i % 4 == 3:
                    head_rstd((i - 7) // 4, P)
            head_rstd(SAMPLE, DEC)
            for m in range(2):
                norm(NT + m, P)

            def hgrn_pre(h):
                if h == 0:
                    act.wait_ge(a_free, mark["proj", 6, SAMPLE])
                f(hfT[:, h, :], hfT[:, h, :], ACT.Exp, scale=-1.0).then_inc(pre_act, 1)
                f(gQ, hqT[:, h, :], ACT.Exp, scale=-1.0).then_inc(pre_act, 1)
                act.wait_ge(pre_dve, 3 * h + 1)
                f(qHat[h % 2], gS, ACT.Ln, bias=lb[:, h:h + 1], scale=oml[:, h:h + 1]).then_inc(pre_act, 1)
                act.wait_ge(pre_dve, 3 * h + 2)
                f(qHat[h % 2], kHat[h % 2], ACT.Exp).then_inc(pre_act, 1)
                f(EB[:, h, :], gB.rearrange("p (b c) -> p b c", c=BLK)[:, :, BLK - 1], ACT.Exp).then_inc(pre_act, 1)
                act.wait_ge(pre_act, 8 * h + 5)
                f(kHat[h % 2], kHat[h % 2], ACT.Exp, scale=-1.0).then_inc(pre_act, 1)
                f(gB, gB, ACT.Exp).then_inc(pre_act, 1)
                f(gE, gE, ACT.Exp).then_inc(pre_act, 1)

            def hgrn_main(h):
                for j in (2 * h, 2 * h + 1):
                    dst = mkN if j < 4 else mvN
                    c = 512 * ((j // 2) % 2)
                    drain(dst[:, j % 2, c:c + 512], lambda b: b[:, :])
                drain(Kt[:, 0:4, :], quads(P))
                drain(Kt[0:DEC, SAMPLE, :], lambda b: b[0:DEC, 0:P])

            def exp_gate(t):
                rows = TILES[t][1]
                if t >= 2:
                    act.wait_ge(sg_ready, t - 1)
                f(eHG[t % 2][0:rows, :], hgN[0:rows, t, :], ACT.Exp, scale=-1.0).then_inc(eg_ready, 1)

            hgrn_pre(0)
            hgrn_pre(1)
            for h in range(H):
                hgrn_main(h)
                exp_gate(h)
                if h + 2 < H:
                    hgrn_pre(h + 2)
            exp_gate(SAMPLE)
            for half in range(2):
                for m in range(2):
                    drain(mkT[:, 4 * half:4 * half + 4, m * P:(m + 1) * P], quads(P))
            for t, (t0, rows) in enumerate(TILES):
                drain(actT[:, 0:4, t0:t0 + rows], quads(rows))
            for t, (t0, rows) in enumerate(TILES):
                head_rstd(NT + t, rows)
            for t, (t0, rows) in enumerate(TILES):
                drain(actT[:, 4:8, t0:t0 + rows], quads(rows))
            for t in range(NT):
                norm(7 + t, TILES[t][1])
            act.wait_ge(sts, 32)
            for half in range(2):
                for m in range(2):
                    drain(cmkT[:, 4 * half:4 * half + 4, m * P:(m + 1) * P], quads(P))
            for u in range(2):
                drain_T(qmT[:, 4 * u:4 * u + 4, :])
            for t in range(NT + 1):
                if t < NT:
                    rows = TILES[t][1]
                    act.wait_ge(mnb_ready, t + 1)
                    for h in range(H):
                        ins = f(Pm[t % 2][0:rows, h, :], pair[0:rows, h // 2, (h % 2) * NMEM:(h % 2 + 1) * NMEM], ACT.Exp,
                                bias=nb[0:rows, t % 2, h:h + 1], scale=MEM_SCALE, accum_out=rs[0:rows, t % 2, h:h + 1])
                    ins.then_inc(mp_ready, 1)
                if t >= 1:
                    rows = TILES[t - 1][1]
                    for half in range(2):
                        drain(pT[:, 4 * half:4 * half + 4, 0:rows], quads(rows))
            for t in range(NT):
                norm(12 + t, TILES[t][1])
            act.wait_ge(r_need, 1)
            f(r_i4, r_t4, ACT.Exp).then_inc(r_exp, 1)
            act.wait_ge(r_need, 2)
            f(r_i, r_i, ACT.Exp).then_inc(r_exp, 1)

            def pair_of_blocks(i):
                for j in range(2):
                    act.wait_ge(gu_full, 2 * i + j + 1)
                    own, other = slice(CAP * j, CAP * (j + 1)), slice(CAP * (1 - j), CAP * (2 - j))
                    f(eG[own, :], banks[1 + j][own, :], ACT.Exp, scale=-1.0)
                    f(eU[own, :], banks[1 + j][other, :], ACT.Copy).then_inc(act_u, 1)
                for j in range(2):
                    act.wait_ge(dn_full, 2 * i + j + 1)
                    if not isinstance(i, int):
                        act.wait_ge(y_st[j], 32 * i)
                    f(yS[j], banks[4 + j][:, :], ACT.Copy).then_inc(y_cp, 1)
                    act.wait_ge(y_cp, 2 * i + j + 1)
                    for half in range(2):
                        act.dma_start(y_dram[bass.ds((2 * i + j) * CAP, CAP), 512 * half:512 * (half + 1)],
                                      yS[j][CAP * half:CAP * (half + 1), :]).then_inc(y_st[j], 16)

            pairs = moe_loops(act, pair_of_blocks)
            for j in range(2):
                act.wait_ge(y_st[j], 32 * (pairs + NE // 2))
            act.sem_inc(y_all, 1)
            for t, (_, rows) in enumerate(TILES):
                act.wait_ge(fssq, t + 1)
                inv_std(rstd[0:rows, 17 + t:18 + t], ssq[0:rows, 17 + t:18 + t], D, frstd)

        @block.vector
        def _(ve):
            v = nc.vector
            n = Chain(ve, dv)
            ts, tt, stt, red = v.tensor_scalar, v.tensor_tensor, v.scalar_tensor_tensor, v.tensor_reduce

            ve.wait_ge(pool_c, 1)
            n.step(v.tensor_copy(tokf, tok_i))
            n.link(v.tensor_copy(dist, dist_i))
            n.link(stt(out=dist, in0=dist, scalar=-1.0, in1=dist, op0=ALU.mult, op1=ALU.max))
            n.step(v.memset(dist[0:64, 448:512], BIG))
            def sum_squares(p, src, hn, rows):
                v.tensor_tensor_reduce(hn[0:rows, :], src, src, 1.0, 0.0, ALU.mult, ALU.add,
                                       ssq[0:rows, p:p + 1]).then_inc(ssq_ready, 1)

            def norm_rows(p, src, hn, rows):
                ve.wait_ge(rstd_ready, p + 1)
                ts(hn[0:rows, :], src, rstd[0:rows, p:p + 1], None, ALU.mult).then_inc(hn_ready, 1)

            def drain_norm(dst, kind, t0, rows):
                for half in range(2):
                    b = V.take(ve)
                    k = slice(4 * half, 4 * half + 4)
                    V.done(tt(dst[:, k, t0:t0 + rows], b[:, :].rearrange("p (c t) -> p c t", c=4)[:, :, 0:rows],
                              gains[:, kind, k].unsqueeze(2).broadcast_to([P, 4, rows]), ALU.mult))

            ve.wait_ge(ldgain, 16)
            for p, (t0, rows) in enumerate(TILES):
                ve.wait_ge(ldx[p % 2], 16 * (p // 2 + 1))
                sum_squares(p, stage1[p % 2][0:rows, :], hn1[p % 2], rows)
                if p:
                    drain_norm(actT, 0, *TILES[p - 1])
                norm_rows(p, stage1[p % 2][0:rows, :], hn1[p % 2], rows)
            drain_norm(actT, 0, *TILES[SAMPLE])
            ve.wait_ge(ldc, 16 * NCONST)
            lp = lamp.rearrange("p (f d) -> p f d", f=4)
            for i in range(2):
                n.step(tt(lamt[:, i, :], lp[:, 2 * i, :], lp[:, 2 * i + 1, :], ALU.mult))
            n.step(tt(lb, lbl[:, 0, :], lbl[:, 1, :], ALU.max))
            n.settle()
            n.step(red(lam[:, 0:2], lamt, AX_X, ALU.add))
            tt(lbl, lbl, lb.unsqueeze(1).broadcast_to([P, 2, H]), ALU.subtract).then_inc(c_in, 1)
            ve.wait_ge(c_exp, 2)
            n.link(tt(oml, lbl[:, 0, :], lbl[:, 1, :], ALU.add))
            n.link(v.reciprocal(oml, oml))
            n.link(tt(lb, lbl[:, 0, :], oml, ALU.mult))
            n.step(ts(oml, lb, -1.0, 1.0, ALU.mult, ALU.add))
            n.link(tt(lam[:, 2:3], lam[:, 1:2], lam[:, 0:1], ALU.subtract))
            n.step(ts(lam[:, 2:3], lam[:, 2:3], -LAM_INIT, None, ALU.add))
            ts(gsub, gsub, 1.0 - LAM_INIT, None, ALU.mult).then_inc(cst, 1)
            ve.wait_ge(cst, 1)


            def soft(i):
                t, h = divmod(i, H)
                rows = TILES[t][1]
                keys, c0 = ((t + 1) * P, SEQ - (t + 1) * P) if t < SAMPLE else (PAST + DEC, 256)
                u = U[i % 3][0:rows, :, 0:keys]
                ve.wait_ge(s_full, i + 1)
                stt(out=u, in0=dist[0:rows, c0:c0 + keys].unsqueeze(1).broadcast_to([rows, 2, keys]), scalar=-SLOPES[h] / DA_SCALE,
                    in1=pair[0:rows, :, 0:keys], op0=ALU.mult, op1=ALU.add).then_inc(s_free, 1)
                ve.wait_ge(s_free, i + 1)
                n.link(red(mx[0:rows, i % 2, 0:2], u, AX_X, ALU.max))
                ts(nb[0:rows, i % 2, 0:2], mx[0:rows, i % 2, 0:2], -DA_SCALE, None, ALU.mult).then_inc(nb_ready, 1)

            def difference(i):
                t, h = divmod(i, H)
                rows = TILES[t][1]
                keys = (t + 1) * P if t < SAMPLE else PAST + DEC
                u = U[i % 3]
                r = rc[0:rows, i % 2, :]
                ve.wait_ge(p_ready, i + 1)
                n.link(v.reciprocal(r[:, 0:2], rs[0:rows, i % 2, 0:2]))
                n.link(tt(r[:, 2:3], r[:, 1:2], lam[0:rows, 2:3], ALU.mult))
                n.link(ts(u[0:rows, 1, 0:keys], u[0:rows, 1, 0:keys], r[:, 2:3], None, ALU.mult))
                stt(out=u[0:rows, 0, 0:keys], in0=u[0:rows, 0, 0:keys], scalar=r[:, 0:1], in1=u[0:rows, 1, 0:keys],
                    op0=ALU.mult, op1=ALU.add).then_inc(w_ready, 1)

            def drain_heads(dst, t, h):
                rows = TILES[t][1]
                b = V.take(ve)
                V.done(v.tensor_copy(dst[0:rows, t, h * P:(h + 1) * P], b[0:rows, 0:P]))

            for i in range(NT * H + 2):
                if i < NT * H:
                    soft(i)
                if i == 2:
                    ve.wait_ge(stk, 32)
                if i >= 2:
                    drain_heads(o_da, *divmod(i - 2, H))
                if i < NT * H:
                    difference(i)

            for m in range(2):
                ve.wait_ge(ldx[(NT + m) % 2], 16 * ((NT + m) // 2 + 1))
                sum_squares(NT + m, stage2[m], hn2[m], P)
                if m:
                    drain_norm(mnT, 1, 0, P)
                norm_rows(NT + m, stage2[m], hn2[m], P)
            drain_norm(mnT, 1, P, P)

            def hgrn_pre(h):
                def blocks(x):
                    return x.rearrange("p (b c) -> p b c", c=BLK)
                F, Q = hfT[:, h, :], hqT[:, h, :]
                k = oml[:, h:h + 1]
                ve.wait_ge(pre_act, 8 * h + 1)
                n.link(ts(gS, F, BIG, 1.0, ALU.min, ALU.add))
                v.reciprocal(gS, gS).then_inc(pre_dve, 1)
                ve.wait_ge(pre_dve, 3 * h + 1)
                n.step(stt(out=F, in0=F, scalar=BIG, in1=gS, op0=ALU.min, op1=ALU.mult))
                ve.wait_ge(pre_act, 8 * h + 2)
                n.link(ts(gQ, gQ, 1.0, None, ALU.add))
                n.link(v.reciprocal(gQ, gQ))
                n.step(tt(Q, Q, gQ, ALU.mult))
                ve.wait_ge(pre_act, 8 * h + 3)
                n.link(v.tensor_tensor_scan(gB, scanm, qHat[h % 2], 0.0, ALU.mult, ALU.add))
                b3 = blocks(gB)
                mid = b3[:, :, BLK // 2 - 1:BLK // 2].broadcast_to([P, NBLK, BLK])
                end = b3[:, :, BLK - 1:BLK].broadcast_to([P, NBLK, BLK])
                n.step(tt(blocks(kHat[h % 2]), b3, mid, ALU.subtract))
                tt(blocks(gE), end, b3, ALU.subtract).then_inc(pre_dve, 1)
                ve.wait_ge(pre_act, 8 * h + 8)
                n.settle()
                n.step(tt(qHat[h % 2], qHat[h % 2], Q, ALU.mult))
                n.step(stt(out=kHat[h % 2], in0=F, scalar=k, in1=kHat[h % 2], op0=ALU.mult, op1=ALU.mult))
                n.settle()
                n.step(tt(Q, Q, gB, ALU.mult))
                stt(out=F, in0=F, scalar=k, in1=gE, op0=ALU.mult, op1=ALU.mult).then_inc(pre_dve, 1)

            def hgrn_main(h):
                b = V.take(ve)
                V.done(v.copy_predicated(PT[:, 0:4, :], bdmask.unsqueeze(1).broadcast_to([P, 4, P]),
                                         b[:, :].rearrange("p (t c) -> p t c", t=4)))
                b = V.take(ve)
                V.done(v.copy_predicated(PT[0:DEC, SAMPLE, 0:DEC], bdmask[0:DEC, 0:DEC], b[0:DEC, 0:DEC]))

                def state(g):
                    if g == SEQ // BLK:
                        return St0[:, h, :]
                    return Sring[:, (h * NBLK + g) % 12, :]

                def update(t):
                    b = V.take(ve)
                    last = TILES[t][1] // BLK - 1
                    for j in range(last + 1):
                        g = 4 * t + j
                        inc = b[:, j * P:(j + 1) * P]
                        dst = SF[:, h, :] if g == SEQ // BLK - 1 else SF[:, H + h, :] if g == NBLK - 1 else state(g + 1)
                        if g == 0:
                            ins = v.tensor_copy(dst, inc)
                        else:
                            if g == SEQ // BLK:
                                ve.wait_ge(ldcache, 48)
                            ins = stt(out=dst, in0=state(g), scalar=EB[:, h, g:g + 1], in1=inc, op0=ALU.mult, op1=ALU.add)
                        if j < last:
                            n.link(ins)
                    V.done(ins)
                    ve.wait_ge(v_free, V.drained)

                update(0)
                for t in range(NT):
                    if t + 1 < NT:
                        update(t + 1)
                    drain_heads(o_hg, t, h)

            def swish_gate(t):
                rows = TILES[t][1]
                e, g = eHG[t % 2][0:rows, :], hgN[0:rows, t, :]
                ve.wait_ge(eg_ready, t + 1)
                n.link(ts(e, e, 1.0, None, ALU.add))
                n.link(v.reciprocal(e, e))
                n.link(tt(g, g, e, ALU.mult))
                g3 = g.rearrange("p (h d) -> p h d", h=H)
                tt(g3, g3, ggn[0:rows, :].unsqueeze(1).broadcast_to([rows, H, P]), ALU.mult).then_inc(sg_ready, 1)

            n.link(v.memset(scanm, 1.0))
            n.link(v.memset(scanm.rearrange("p (b c) -> p b c", c=BLK)[:, :, 0:1], 0.0))
            hgrn_pre(0)
            hgrn_pre(1)
            for h in range(H):
                hgrn_main(h)
                swish_gate(h)
                if h + 2 < H:
                    hgrn_pre(h + 2)
            swish_gate(SAMPLE)

            def add_rows(p0, kind, dst, stored):
                for t, (t0, rows) in enumerate(TILES):
                    for half in range(2):
                        c = slice(512 * half, 512 * (half + 1))
                        b = V.take(ve)
                        V.done(tt(x_sb[0:rows, t, c], x_sb[0:rows, t, c], b[0:rows, :], ALU.add))
                    ve.wait_ge(v_free, V.drained)
                    if stored and t >= 2:
                        ve.wait_ge(hn_st[t % 2], 16 * (t // 2))
                    sum_squares(p0 + t, x_sb[0:rows, t, :], hn3[t % 2], rows)
                    if t:
                        drain_norm(dst, kind, *TILES[t - 1])
                    norm_rows(p0 + t, x_sb[0:rows, t, :], hn3[t % 2], rows)
                drain_norm(dst, kind, *TILES[SAMPLE])

            ve.wait_ge(ldxr, 32)
            add_rows(7, 2, hmT, False)
            for t in range(NT + 1):
                if t < NT:
                    rows = TILES[t][1]
                    m, q = mx[0:rows, t % 2, :], rc[0:rows, t % 2, :]
                    ve.wait_ge(s_full, NT * H + t + 1)
                    n.link(red(m, pair[0:rows].rearrange("p b (q m) -> p (b q) m", q=2), AX_X, ALU.max))
                    ts(nb[0:rows, t % 2, :], m, -MEM_SCALE, None, ALU.mult).then_inc(mnb_ready, 1)
                    ve.wait_ge(mp_ready, t + 1)
                    n.link(v.reciprocal(q, rs[0:rows, t % 2, :]))
                    pm = Pm[t % 2][0:rows, :, :]
                    tt(pm, pm, q.unsqueeze(2).broadcast_to([rows, H, NMEM]), ALU.mult).then_inc(mpn_ready, 1)
                if t >= 1:
                    t0, rows = TILES[t - 1]
                    for half in range(2):
                        b = V.take(ve)
                        V.done(v.tensor_copy(actT[:, 4 * half:4 * half + 4, t0:t0 + rows],
                                             b[:, :].rearrange("p (c t) -> p c t", c=4)[:, :, 0:rows]))
            add_rows(12, 3, hmT, True)

            def wide(x, w):
                return x.unsqueeze(2).broadcast_to([P, NT, w])

            def over_tiles(x, w):
                return x.unsqueeze(1).broadcast_to([P, NT, w])

            n.step(v.memset(lg, 0.0))
            n.step(v.tensor_copy(iota32, iota_i[:, 0:NE]))
            n.step(v.tensor_copy(iota_s, iota_i))
            n.step(v.memset(ones32, 1.0))
            n.step(v.memset(ovf, 0.0))
            n.settle()
            n.step(ts(e64, iota32, float(CAP), None, ALU.mult))
            for t, (_, rows) in enumerate(TILES):
                b = V.take(ve)
                V.done(tt(lg[0:rows, t, :], b[0:rows, 0:36], rbias[0:rows, :], ALU.add))
            ve.wait_ge(v_free, V.drained)
            n.settle()
            glog = lg[:, :, 0:GROUPS]
            n.link(red(r_g1, glog, AX_X, ALU.max))
            tt(r_t4, glog, wide(r_g1, GROUPS), ALU.subtract).then_inc(r_need, 1)
            ve.wait_ge(r_exp, 1)
            n.step(red(r_sum, r_i4, AX_X, ALU.add))
            n.settle()
            n.step(v.reciprocal(r_sum, r_sum))

            def first_best(hot, x, best, work, width, io):
                n.link(tt(work, x, wide(best, width), ALU.is_equal))
                n.link(stt(out=work, in0=work, scalar=-1000.0, in1=over_tiles(io, width), op0=ALU.mult, op1=ALU.add))
                n.link(red(r_i, work, AX_X, ALU.min))
                n.link(tt(hot, work, wide(r_i, width), ALU.is_equal))

            first_best(r_i4, glog, r_g1, r_t4, GROUPS, iota32[:, 0:GROUPS])
            n.link(ts(r_i4, r_i4, -1.0, BIG, ALU.add, ALU.mult))
            for g in range(GROUPS):
                s = slice(g * PER_GROUP, (g + 1) * PER_GROUP)
                n.step(tt(r_e[:, :, s], lg[:, :, GROUPS + g * PER_GROUP:GROUPS + (g + 1) * PER_GROUP],
                          r_i4[:, :, g:g + 1].broadcast_to([P, NT, PER_GROUP]), ALU.add))
            n.settle()
            for k in range(2):
                n.link(red(r_v[k], r_e, AX_X, ALU.max))
                first_best(r_oh[k], r_e, r_v[k], r_t, NE, iota32)
                if k == 0:
                    n.link(stt(out=r_e, in0=r_oh[0], scalar=-2.0 * BIG, in1=r_e, op0=ALU.mult, op1=ALU.add))
            n.link(tt(r_sel, r_oh[0], r_oh[1], ALU.add))
            v.memset(r_sel[DEC:P, SAMPLE, :], 0.0).then_inc(sel_ready, 1)
            n.step(tt(r_i, r_v[1], r_v[0], ALU.subtract))
            v.memset(gate[0], 0.0).then_inc(r_need, 1)
            ve.wait_ge(r_exp, 2)
            n.settle()
            n.link(ts(gate[1], r_i, 1.0, None, ALU.add))
            n.link(v.reciprocal(gate[1], gate[1]))
            n.link(tt(gate[0], gate[1], r_sum, ALU.mult))
            n.link(tt(gate[1], gate[0], r_i, ALU.mult))
            b = V.take(ve)
            V.done(v.tensor_copy(rank_cnt, b[:, 0:(NT + 1) * NE]))
            ve.wait_ge(v_free, V.drained)
            for k in range(1, -(-TOK // CAP)):
                n.link(stt(out=ovf, in0=cnt, scalar=float(CAP * k), in1=ovf, op0=ALU.is_gt, op1=ALU.add))
            n.link(v.tensor_tensor_scan(cum, ones32, ovf, 0.0, ALU.mult, ALU.add))
            n.link(tt(base, cum, ovf, ALU.subtract))
            n.link(ts(base, base, float(CAP), float(CAP * (NE - 1)), ALU.mult, ALU.add))
            n.link(tt(base, base, e64, ALU.subtract))
            for k in range(2):
                for out, table in ((r_R, rank), (r_E, over_tiles(e64, NE)), (r_O, over_tiles(base, NE))):
                    n.link(tt(r_t, r_oh[k], table, ALU.mult))
                    n.link(red(out, r_t, AX_X, ALU.add))
                n.link(stt(out=r_O, in0=r_R, scalar=float(CAP), in1=r_O, op0=ALU.is_ge, op1=ALU.mult))
                n.link(tt(r_E, r_E, r_O, ALU.add))
                n.link(tt(slotf[:, k, :], r_E, r_R, ALU.add))
            v.tensor_copy(slot_i, slotf).then_inc(slot_ready, 1)
            ve.wait_ge(slot_ready, 1)
            n.step(ts(lo_i, slot_i, 2 * CAP - 1, None, ALU.bitwise_and))
            n.step(ts(hi_i, slot_i, 7, None, ALU.arith_shift_right))
            n.settle()
            n.step(v.tensor_copy(lo_f, lo_i))
            n.step(v.tensor_copy(hi_f, hi_i))
            n.settle()
            for k in range(2):
                n.step(tt(hot_s[k], over_tiles(iota_s, 2 * CAP), wide(lo_f[:, k, :], 2 * CAP), ALU.is_equal))
                n.link(tt(hot_p[k], over_tiles(iota_s[:, 0:NB // 2], NB // 2), wide(hi_f[:, k, :], NB // 2), ALU.is_equal))
                ins = tt(hot_p[k], hot_p[k], wide(tokf, NB // 2), ALU.mult)
                if k == 0:
                    n.step(ins)
            ins.then_inc(hot_ready, 1)
            b = V.take(ve)
            V.done(v.tensor_copy(sidx, b[:, 0:NB // 2]))
            n.step(tt(cmp_e, cum.unsqueeze(1).broadcast_to([P, OVER, NE]),
                      iota32[:, 0:OVER].unsqueeze(2).broadcast_to([P, OVER, NE]), ALU.is_le))
            n.step(ts(cmp_p[:, 0:OVER // 2], iota32[:, 0:OVER:2], cum[:, NE - 1:NE], None, ALU.is_lt))
            n.settle()
            n.step(red(eo, cmp_e, AX_X, ALU.add))
            n.step(red(npf, cmp_p[:, 0:OVER // 2], AX_X, ALU.add))
            n.settle()
            n.link(ts(eo, eo, float(NE - 1), None, ALU.min))
            n.step(v.tensor_copy(meta_i, eo))
            v.tensor_copy(np_i, npf).then_inc(meta_ready, 1)

            def pair_of_blocks(i):
                ve.wait_ge(tx_full, i + 1)
                for half in range(2):
                    k = slice(4 * half, 4 * half + 4)
                    ins = tt(xgT[:, k, :], pair[:, half, :].rearrange("p (k t) -> p k t", k=4),
                             gains[:, 3, k].unsqueeze(2).broadcast_to([P, 4, P]), ALU.mult)
                ins.then_inc(xT_cp, 1)
                for j in range(2):
                    own = slice(CAP * j, CAP * (j + 1))
                    ve.wait_ge(act_u, 2 * i + j + 1)
                    tt(eU[own, :], banks[1 + j][own, :], eU[own, :], ALU.mult).then_inc(mdv, 1)
                ts(eG, eG, 1.0, None, ALU.add).then_inc(mdv, 1)
                ve.wait_ge(mdv, 4 * i + 3)
                v.reciprocal(eG, eG).then_inc(mdv, 1)
                ve.wait_ge(mdv, 4 * i + 4)
                tt(hE, eU, eG, ALU.mult).then_inc(hE_ready, 1)
                ve.wait_ge(th_full, i + 1)
                v.tensor_copy(hET, banks[3][:, :].rearrange("p (k t) -> p k t", k=4)).then_inc(hT_cp, 1)

            moe_loops(ve, pair_of_blocks)
            for t, (t0, rows) in enumerate(TILES):
                o = fin[t % 2][0:rows, :]
                ve.wait_ge(yg_ld[t], 32)
                if t >= 2:
                    ve.wait_ge(fin_st[t % 2], 16 * (t // 2))
                n.link(stt(out=o, in0=yg[t][0][0:rows, :], scalar=gate[0][0:rows, t:t + 1], in1=x_sb[0:rows, t, :],
                           op0=ALU.mult, op1=ALU.add))
                n.link(stt(out=o, in0=yg[t][1][0:rows, :], scalar=gate[1][0:rows, t:t + 1], in1=o,
                           op0=ALU.mult, op1=ALU.add))
                v.tensor_tensor_reduce(fjunk[0:rows, :], o, o, 1.0, 0.0, ALU.mult, ALU.add,
                                       ssq[0:rows, 17 + t:18 + t]).then_inc(fssq, 1)
                ve.wait_ge(frstd, t + 1)
                stt(out=o, in0=o, scalar=rstd[0:rows, 17 + t:18 + t], in1=gfin[0:rows, :], op0=ALU.mult,
                    op1=ALU.mult).then_inc(fin_ready, 1)


_INS = ["x_prompt", "x_sample", "mem_prompt", "cache_diff_k", "cache_diff_v", "state_hgrn", "cache_mem_k", "cache_mem_v",
        "ln_mix_g", "w_in", "da_lambda", "da_subln_g", "hg_lb_logits", "hg_gnorm_g", "w_out", "ln_mem_g", "mem_norm_g",
        "w_mem_q", "w_mem_k", "w_mem_v", "w_mem_o", "ln_ffn_g", "router_group_w", "router_group_b", "router_expert_w",
        "router_expert_b", "exp_w_gate", "exp_w_up", "exp_w_down", "final_norm_g"]
_OUTS = [(1, 512, 1024), (1, 64, 1024), (1, 1, 512, 4, 128), (1, 1, 512, 4, 128), (1, 1, 4, 128, 128),
         (1, 1, 256, 4, 256), (1, 1, 256, 4, 256), (1, 1, 64, 4, 128), (1, 1, 64, 4, 128), (1, 1, 4, 128, 128)]


def kernel(**inputs):
    import numpy as _np
    import concourse.bacc as _bacc
    from concourse import mybir as _mybir
    from concourse.bass_utils import run_bass_kernel_spmd as _run

    nc = _bacc.Bacc("TRN2", target_bir_lowering=False, num_devices=1)
    arrays, args, outs = {}, {}, []
    for name in _INS:
        x = _np.ascontiguousarray(inputs[name])
        arrays[f"in_{name}_dram"] = x
        args[name] = nc.dram_tensor(f"in_{name}_dram", x.shape, _mybir.dt.from_np(x.dtype), kind="ExternalInput").ap()
    for i, shape in enumerate(_OUTS):
        outs.append(nc.dram_tensor(f"out_{i}_dram", shape, _mybir.dt.float32, kind="ExternalOutput").ap())
    encoder(nc, args, outs)
    r = _run(nc, [arrays], core_ids=[0])
    return tuple(r.results[0][f"out_{i}_dram"] for i in range(len(_OUTS)))
```

```python
from contextlib import ExitStack

import concourse.bass as bass
from concourse import mybir

F32 = mybir.dt.float32
I32 = mybir.dt.int32
U32 = mybir.dt.uint32
ALU = mybir.AluOpType
ACT = mybir.ActivationFunctionType
AX_X = mybir.AxisListType.X

P = 128
D = 1024
KC = D // P
SEQ, DEC, PAST, NMEM = 512, 64, 128, 256
TOK = SEQ + DEC
TILES = [(t * P, P) for t in range(SEQ // P)] + [(SEQ, DEC)]
NT = len(TILES)
SAMPLE = NT - 1
H = 4
DA_SCALE = 64 ** -0.5
LAM_INIT = 0.8 - 0.6
SLOPES = [2.0 ** (-2 * (h + 1)) for h in range(H)]
MEM_SCALE = 256 ** -0.5
EPS = 1e-5
BLK = 32
NBLK = TOK // BLK
HALF = TOK // 2
T_JOBS = [(c, HALF * half) for half in range(2) for c in range(4)]
GROUPS, PER_GROUP = 4, 8
NE = GROUPS * PER_GROUP
FF = 512
CAP = 64
MAX_OVER = (2 * TOK - 1) // CAP
OVER = MAX_OVER + MAX_OVER % 2
NB = NE + OVER
BIG = 1.0e30


class PsumRing:

    def __init__(self, banks, full, free):
        self.banks, self.full, self.free = banks, full, free
        self.filled = self.drained = 0

    def open(self, pe):
        n = len(self.banks)
        if self.filled >= n:
            pe.wait_ge(self.free, self.filled - n + 1)
        return self.banks[self.filled % n]

    def close(self, ins):
        ins.then_inc(self.full, 1)
        self.filled += 1
        return self.filled

    def take(self, eng):
        eng.wait_ge(self.full, self.drained + 1)
        return self.banks[self.drained % len(self.banks)]

    def done(self, ins):
        ins.then_inc(self.free, 1)
        self.drained += 1
        return self.drained


class Chain:

    def __init__(self, eng, sem):
        self.eng, self.sem, self.n = eng, sem, 0

    def step(self, ins):
        ins.then_inc(self.sem, 1)
        self.n += 1

    def settle(self):
        self.eng.wait_ge(self.sem, self.n)

    def link(self, ins):
        self.step(ins)
        self.settle()


def encoder(nc, a, outs):
    (y_prompt, y_sample, nk_p, nv_p, ns_p, nmk, nmv, nk_s, nv_s, ns_s) = outs
    hn_dram = nc.dram_tensor("hn_rows", (TOK, D), F32).ap()
    y_dram = nc.dram_tensor("expert_rows", (NB * CAP, D), F32).ap()

    with ExitStack() as ctx:
        def sem(name):
            return ctx.enter_context(nc.semaphore(name))

        WORDS = 52944
        arena = ctx.enter_context(nc.sbuf_tensor("arena", [P, WORDS], F32))
        ints = ctx.enter_context(nc.sbuf_tensor("ints", [P, 256], I32))
        banks = [ctx.enter_context(nc.psum_tensor(f"bank{i}", [P, 512], F32)) for i in range(6)]
        pair = ctx.enter_context(nc.psum_tensor("score_pair", [P, 2, 512], F32))

        def area(at, *shape, dt=None):
            n = 1
            for s in shape:
                n *= s
            v = arena[:, at:at + n]
            if dt is not None:
                v = v.bitcast(dt)
            if len(shape) == 2:
                v = v.rearrange("p (a b) -> p a b", a=shape[0])
            if len(shape) == 3:
                v = v.rearrange("p (a b c) -> p a b c", a=shape[0], b=shape[1])
            return v

        RING = 0
        NSLOT = 2
        KHZ = RING + NSLOT * 4096
        Z1 = KHZ + 4096
        Z2 = Z1 + 8192
        MZ = Z2 + 9728
        AZ = MZ + 5120
        XZ = AZ + 4608
        OZ = XZ + 5120
        CZ = OZ + 5376

        wslot = [area(RING + 4096 * s, KC, 512) for s in range(NSLOT)]
        qT = area(Z1, H, TOK)
        kT = area(Z1 + 2304, H, TOK)
        ckT = area(Z1 + 4608, H, PAST)
        vN = area(Z1 + 5120, NT, 512)
        cvN = area(Z1 + 7680, 512)
        hqT = area(Z2, H, TOK)
        hfT = area(Z2 + 2304, H, TOK)
        hiN = area(Z2 + 4608, NT, 512)
        hgN = area(Z2 + 7168, NT, 512)
        kN = area(MZ, NT, 512)
        o_da = area(MZ, NT, 512)
        ckN = area(MZ + 2560, 512)
        o_hg = area(MZ + 2560, NT, 512)
        actT = area(AZ, KC, TOK)
        U = [area(XZ + 1024 * i, 2, 512) for i in range(3)]
        wT = [area(XZ + 3072 + 512 * i, 4, P) for i in range(2)]
        stage1 = [area(Z2 + 1024 * i, 1024) for i in range(4)] + [area(MZ, 1024)]
        hn1 = [area(Z2 + 5120 + 1024 * i, 1024) for i in range(2)]
        squares = area(Z2 + 7168, 1024)
        eHG = [area(AZ + 512 * i, 512) for i in range(NT)]
        gS, gB, gE, gQ = (area(XZ + TOK * i, TOK) for i in range(4))
        kHat = [area(KHZ + TOK * h, TOK) for h in range(H)]
        qHat = [area(KHZ + TOK * (H + h), TOK) for h in range(H - 1)] + [area(XZ + 4096, TOK)]
        Vbd = area(OZ, NT, 4, P)
        Kt = area(OZ + 2560, NT, P)
        PT = area(OZ + 3200, NT, P)
        Sring = area(OZ + 3840, 12, P)
        stage2 = [area(MZ + 2560 + 1024 * i, 1024) for i in range(2)]
        hn2 = [area(OZ + 3840, 1024), stage2[1]]
        mkN = area(XZ, 2, 1024)
        mkT = area(Z1, KC, NMEM)
        mvN = area(Z1 + 2048, 2, 1024)
        mnT = area(Z1 + 4096, KC, NMEM)
        cmkT = area(Z1 + 6144, KC, NMEM)
        St0 = area(Z1 + 6144, H, P)
        SF = area(Z1 + 6656, 2 * H, P)
        x_sb = area(XZ, NT, 1024)
        hmT = area(Z2, KC, TOK)
        qmT = area(Z2 + 4608, KC, TOK)
        hn3 = [area(MZ + 1024 * i, 1024) for i in range(2)]
        cmvN = area(MZ + 2048, 2, 1024)
        Pm = [area(MZ + 4096, H, NMEM), area(OZ + 3072, H, NMEM)]
        cmkN = area(OZ, 2, 1024)
        pT = area(OZ + 2048, KC, P)
        E0 = Z1
        wexp = [[area(RING + 4096 * s, KC, 512) for s in range(2)] + [area(RING + 8192, 4, 1024)],
                [area(E0 + 4096 * s, KC, 512) for s in range(2)] + [area(E0 + 8192, 4, 1024)]]
        MB = E0 + 12288
        xg = area(MB, 1024)
        xgT = area(MB + 1024, KC, 2 * CAP)
        eG = area(MB + 2048, 512)
        eU = area(MB + 2560, 512)
        hE = area(MB + 3072, 512)
        hET = area(MB + 3584, 4, 2 * CAP)
        yS = [area(MB + 4096 + 512 * i, 512) for i in range(2)]
        yg = [[area(Z1 + 1024 * (2 * t + k), 1024) for k in range(2)] for t in range(NT)]
        fin = [area(Z1 + 10240 + 1024 * i, 1024) for i in range(3)]
        rw = area(MZ + 2048, KC, 36)
        gfin = area(MZ + 2336, 1024)
        at = [CZ]

        def small(*shape, dt=None):
            n = 1
            for s in shape:
                n *= s
            at[0] += n
            return area(at[0] - n, *shape, dt=dt)

        scanm = small(TOK)
        dist = scanm[:, 0:512]
        ident = small(P)
        ones = small(P)
        upper = small(P)
        bdmask = small(P, dt=I32)
        gains = small(4, KC)
        gsub = small(P)
        ggn = small(P)
        sq = small(512)
        lamp = sq[:, 0:256]
        lamt = sq[:, 256:384].rearrange("p (a b) -> p a b", a=2)
        lam = small(4)
        lbl = small(2, H)
        lb = small(H)
        oml = small(H)
        neghalf = small(1)
        ssq = small(24)
        rstd = small(24)
        mx = small(2, 4)
        nb = small(2, 4)
        rs = small(2, 4)
        rc = small(2, 4)
        EB = small(H, NBLK)
        hss = small(NT, H)
        hrs = small(NT, H)
        gss = small(H, NT)
        grs = small(H, NT)
        rbias = small(36)
        tokf = small(NT)
        assert at[0] <= WORDS, at[0]
        RZ = [OZ]

        def route(*shape, dt=None):
            n = 1
            for s in shape:
                n *= s
            RZ[0] += n
            return area(RZ[0] - n, *shape, dt=dt)

        lg = route(NT, 36)
        r_g1 = route(NT)
        r_sum = route(NT)
        r_t4 = route(NT, 4)
        r_i4 = route(NT, 4)
        r_e = route(NT, NE)
        r_t = route(NT, NE)
        r_oh = [route(NT, NE) for _ in range(2)]
        r_sel = route(NT, NE)
        before = route(NT + 1, NE)
        place = route(NT, NE)
        r_hit = route(2, NT, NE)
        cnt_i = ints[:, 48:48 + NE]
        r_v = [route(NT) for _ in range(2)]
        r_i = route(NT)
        gate = [route(NT) for _ in range(2)]
        iota32 = route(NE)
        rank_cnt = route((NT + 1) * NE)
        rank = rank_cnt[:, 0:NT * NE].rearrange("p (t e) -> p t e", t=NT)
        cnt = rank_cnt[:, NT * NE:]
        ovf = route(NE)
        cum = route(NE)
        base = route(NE)
        e64 = route(NE)
        ones32 = route(NE)
        slotf = route(2, NT)
        cmp_e = route(OVER, NE)
        eo = route(OVER)
        cmp_p = route(OVER)
        npf = route(1)
        iota_s = route(2 * CAP)
        hot_s = [route(NT, 2 * CAP) for _ in range(2)]
        hot_p = [route(NT, NB // 2) for _ in range(2)]
        lo_f = route(2, NT)
        hi_f = route(2, NT)
        assert RZ[0] <= CZ, RZ[0]
        slot_i = ints[:, 0:2 * NT].rearrange("p (k t) -> p k t", k=2)
        meta_i = ints[:, 16:16 + OVER]
        np_i = ints[:, 40:41]
        over_i = ints[:, 41:42]
        sidx = ints[:, 48:48 + NB // 2]
        gidx = ints[:, 100:101]
        gdum = ints[:, 104:108]
        iota_i = ints[:, 108:108 + 2 * CAP]
        tok_i = ints[:, 236:236 + NT]
        lo_i = ints[:, 80:80 + 2 * NT].rearrange("p (k t) -> p k t", k=2)
        hi_i = ints[:, 90:90 + 2 * NT].rearrange("p (k t) -> p k t", k=2)
        dist_i = area(Z2 + 8192, 512, dt=I32)

        ldgain, ldc = sem("first_gain_loaded"), sem("small_loads")
        ldx = [sem(f"x_stage_loaded{i}") for i in range(NT)]
        ldw = [sem(f"w_slot_loaded{i}") for i in range(NSLOT)]
        ldcache = sem("caches_loaded")
        ldcm = sem("mem_cache_loaded")
        ldxr = sem("x_reloaded")
        ldrt = sem("router_loaded")
        pool_c = sem("pool_constants")
        pool_s = sem("pool_steps")
        cst = sem("vector_constants")
        dv = sem("vector_chain")
        ac = sem("scalar_chain")
        c_in, c_exp = sem("constant_exp_input"), sem("constant_exp")
        a_full, a_free = sem("a_bank_full"), sem("a_bank_drained")
        v_full, v_free = sem("v_bank_full"), sem("v_bank_drained")
        s_full, s_free = sem("score_pair_full"), sem("score_pair_read")
        ssq_ready, rstd_ready, hn_ready = sem("ssq_ready"), sem("rstd_ready"), sem("hn_ready")
        nb_ready, p_ready, w_ready = sem("neg_max_ready"), sem("probs_ready"), sem("diff_weights_ready")
        mix_ready = sem("mixed_ready")
        pre_act, pre_dve = sem("hgrn_pre_scalar"), sem("hgrn_pre_vector")
        vbd_ready = sem("v_blocks_ready")
        eg_ready, sg_ready = sem("exp_gate_ready"), sem("swish_gate_ready")
        mnb_ready, mp_ready, mpn_ready = sem("mem_neg_max"), sem("mem_probs"), sem("mem_probs_scaled")
        hn_st = [sem(f"hn_rows_stored{i}") for i in range(2)]
        stk, stv, sts, stmk, stmv = (sem(f"stored_{n}") for n in ("k", "v", "state", "mem_k", "mem_v"))
        r_exp = sem("router_exp")
        r_need = sem("router_exp_input")
        sel_ready, slot_ready, meta_ready = sem("selection_ready"), sem("slots_ready"), sem("meta_ready")
        y_zero = sem("spare_rows_zeroed")
        hot_ready = sem("slot_one_hots_ready")
        ldg = [sem(f"w_gate_loaded{j}") for j in range(2)]
        ldu = [sem(f"w_up_loaded{j}") for j in range(2)]
        ldd = [sem(f"w_down_loaded{j}") for j in range(2)]
        xg_ld = sem("rows_gathered")
        gi_ready = sem("gather_index_ready")
        tx_full, gu_full, th_full, dn_full = (sem(n) for n in ("xT_in_psum", "gate_up_done", "hT_in_psum", "down_done"))
        xT_cp, hE_ready, hT_cp, y_cp = (sem(n) for n in ("xT_copied", "h_ready", "hT_copied", "y_copied"))
        act_u, mdv = sem("exp_and_up_copied"), sem("moe_vector_chain")
        y_st = [sem(f"y_rows_stored{j}") for j in range(2)]
        y_all = sem("all_y_stored")
        yg_ld = [sem(f"y_rows_gathered{t}") for t in range(NT)]
        fsum, fssq, frstd, fin_ready = (sem(f"final_{n}") for n in ("sum", "ssq", "rstd", "ready"))
        fin_st = [sem(f"final_stored{i}") for i in range(3)]

        A = PsumRing(banks[0:3], a_full, a_free)
        V = PsumRing(banks[3:6], v_full, v_free)
        mark = {}

        UNITS = [("w_in", 512 * c) for c in (4, 3, 0, 1, 2, 5, 6)]
        UNITS += [("w_mem_k", 0), ("w_mem_k", 512), ("w_mem_v", 0), ("w_mem_v", 512)]
        UNITS += [("w_out", 0), ("w_out", 512), ("w_mem_q", 0), ("w_mem_q", 512), ("w_mem_o", 0), ("w_mem_o", 512)]
        unit_done = {}
        jobs = [(4 + j % 2, j // 2) for j in range(2 * NT)] + [(6, t) for t in range(NT)]
        steps = [0, 3] + list(range(5, 18))
        FILL = dict(zip(steps, jobs))
        NCONST = 9

        block = ctx.enter_context(nc.Block())

        def moe_loops(eng, body):
            body(0)
            with eng.Fori(1, NE // 2) as i:
                body(i)
            eng.wait_ge(meta_ready, 1)
            pairs = eng.value_load(np_i[0:1, 0:1], min_val=0, max_val=OVER // 2)
            with eng.If(pairs > 0):
                with eng.Fori(NE // 2, pairs + NE // 2) as i:
                    body(i)
            return pairs

        @block.tensor
        def _(pe):
            mm, tr = nc.tensor.matmul, nc.tensor.transpose
            pe.wait_ge(pool_c, 1)

            def norm(n, hn, rows):
                pe.wait_ge(hn_ready, n + 1)
                for half in range(2):
                    b = V.open(pe)
                    for c in range(4):
                        k = 4 * half + c
                        ins = tr(b[:, c * P:c * P + rows], hn[0:rows, k * P:(k + 1) * P], ident[0:rows, 0:rows])
                    mark["norm", n, half] = V.close(ins)

            def weights(u):
                pe.wait_ge(ldw[u % NSLOT], 16 * (u // NSLOT + 1))
                return wslot[u % NSLOT]

            def proj_T(u, src, j):
                w = weights(u)
                c, t0 = T_JOBS[j]
                b = A.open(pe)
                for k in range(KC):
                    ins = mm(b[:, 0:HALF], w[:, k, c * P:(c + 1) * P], src[:, k, t0:t0 + HALF], start=k == 0, stop=k == KC - 1)
                unit_done[u] = (a_full, A.close(ins))
                mark["proj", u, j] = A.filled

            def proj_N(u, src, t, ring, tiles=TILES):
                w = weights(u)
                t0, rows = tiles[t]
                b = ring.open(pe)
                for k in range(KC):
                    x = src[:, k, t0:t0 + rows]
                    if rows == P:
                        ins = mm(b[:, :], x, w[:, k, :], start=k == 0, stop=k == KC - 1)
                    else:
                        for half in range(2):
                            ins = mm(b[rows * half:rows * (half + 1), 0:256], x, w[:, k, 256 * half:256 * (half + 1)],
                                     start=k == 0, stop=k == KC - 1)
                unit_done[u] = (ring.full, ring.close(ins))
                mark["proj", u, t] = ring.filled

            for n in range(3):
                norm(n, hn1[n % 2], P)
            for u in range(3):
                for j, (c, t0) in enumerate(T_JOBS):
                    if u == 0 and c == 0:
                        pe.wait_ge(v_free, mark["norm", 2 if t0 == 0 else SAMPLE, 1])
                    proj_T(u, actT, j)
                    if u == 0 and j < 2:
                        norm(3 + j, hn1[(3 + j) % 2], TILES[3 + j][1])
            for t in range(NT):
                proj_N(3, actT, t, A)
            for t in range(NT):
                rows = TILES[t][1]
                b = A.open(pe)
                pe.wait_ge(a_free, mark["proj", 3, t])
                for h in range(H):
                    ins = tr(b[:, h * P:h * P + rows], kN[0:rows, t, h * P:(h + 1) * P], ident[0:rows, 0:rows])
                mark["kT", t] = A.close(ins)
            b = A.open(pe)
            pe.wait_ge(ldcache, 32)
            for h in range(H):
                ins = tr(b[:, h * P:(h + 1) * P], ckN[:, h * P:(h + 1) * P], ident)
            mark["ckT"] = A.close(ins)

            def scores(i):
                t, h = divmod(i, H)
                t0, rows = TILES[t]
                if i == 0:
                    pe.wait_ge(a_free, mark["ckT"])
                if i >= 1:
                    pe.wait_ge(s_free, i)
                for c in range(2):
                    lo = 64 * c
                    q = qT[lo:lo + 64, h, t0:t0 + rows]
                    if t < SAMPLE:
                        ins = mm(pair[0:rows, c, 0:t0 + P], q, kT[lo:lo + 64, h, 0:t0 + P], start=True, stop=True)
                    else:
                        mm(pair[0:rows, c, 0:PAST], q, ckT[lo:lo + 64, h, :], start=True, stop=True)
                        ins = mm(pair[0:rows, c, PAST:PAST + DEC], q, kT[lo:lo + 64, h, SEQ:TOK], start=True, stop=True)
                ins.then_inc(s_full, 1)

            def key_blocks(t):
                if t < SAMPLE:
                    return [(P * j, P) for j in range(t + 1)]
                return [(0, PAST), (PAST, DEC)]

            def turn_weights(i):
                t, h = divmod(i, H)
                rows = TILES[t][1]
                pe.wait_ge(w_ready, i + 1)
                b = A.open(pe)
                for j, (k0, n) in enumerate(key_blocks(t)):
                    ins = tr(b[0:n, j * P:j * P + rows], U[i % 3][0:rows, 0, k0:k0 + n], ident[0:rows, 0:rows])
                mark["wT", i] = A.close(ins)

            def weigh_values(i):
                t, h = divmod(i, H)
                rows = TILES[t][1]
                pe.wait_ge(a_free, mark["wT", i])
                if h == 0:
                    pe.wait_ge(a_free, mark["proj", 4, t])
                b = A.open(pe)
                kb = key_blocks(t)
                for j, (k0, n) in enumerate(kb):
                    if t < SAMPLE:
                        v = vN[:, j, h * P:(h + 1) * P]
                    else:
                        v = cvN[:, h * P:(h + 1) * P] if j == 0 else vN[0:n, SAMPLE, h * P:(h + 1) * P]
                    ins = mm(b[0:rows, 0:P], wT[i % 2][0:n, j, 0:rows], v, start=j == 0, stop=j == len(kb) - 1)
                mark["o_da", t] = A.close(ins)

            for i in range(NT * H + 3):
                if i < NT * H:
                    scores(i)
                if i in FILL:
                    proj_N(FILL[i][0], actT, FILL[i][1], A)
                if 2 <= i <= NT * H + 1:
                    turn_weights(i - 2)
                if i >= 3:
                    weigh_values(i - 3)

            MT = [(0, P), (P, P)]
            for m in range(2):
                norm(NT + m, hn2[m], P)
            pe.wait_ge(v_free, mark["norm", NT + 1, 1])

            def mem_kv(j):
                proj_N(7 + j // 2, mnT, j % 2, A, MT)

            def hgrn(h):
                pe.wait_ge(pre_dve, 3 * h + 3)
                b = V.open(pe)
                for t in range(4):
                    s = slice(t * P, (t + 1) * P)
                    ins = mm(b[:, t * P:(t + 1) * P], kHat[h][:, s], qHat[h][:, s], start=True, stop=True)
                V.close(ins)
                b = V.open(pe)
                ins = mm(b[0:DEC, 0:DEC], kHat[h][:, SEQ:TOK], qHat[h][:, SEQ:TOK], start=True, stop=True)
                mark["PT", h] = V.close(ins)
                b = A.open(pe)
                for t in range(4):
                    ins = tr(b[:, t * P:(t + 1) * P], hfT[:, h, t * P:(t + 1) * P], ident)
                A.close(ins)
                b = A.open(pe)
                mark["Kt", h] = A.close(tr(b[0:DEC, 0:P], hfT[:, h, SEQ:TOK], ident))
                state_at = {}

                def increments(t):
                    rows = TILES[t][1]
                    nb4 = rows // BLK
                    if t == 0:
                        pe.wait_ge(vbd_ready, h + 1)
                        pe.wait_ge(a_free, mark["Kt", h])
                    b = V.open(pe)
                    ins = mm(b[:, 0:nb4 * P].rearrange("p (j v) -> p j v", j=nb4), Kt[0:rows, t, :],
                             Vbd[0:rows, t, 0:nb4, :], start=True, stop=True)
                    state_at[t] = V.close(ins)
                    mark["G", h, t] = V.filled

                def outputs(t):
                    t0, rows = TILES[t]
                    if t == 0:
                        pe.wait_ge(v_free, mark["PT", h])
                    pe.wait_ge(v_free, state_at[t])
                    if t == SAMPLE:
                        pe.wait_ge(ldcache, 48)
                    b = A.open(pe)
                    ins = mm(b[0:rows, 0:P], PT[0:rows, t, 0:rows], hiN[0:rows, t, h * P:(h + 1) * P],
                             start=True, stop=False, skip_group_check=True)
                    for j in range(rows // BLK):
                        g = 4 * t + j
                        if g == 0:
                            continue
                        s0 = St0[:, h, :] if t == SAMPLE and j == 0 else Sring[:, (h * NBLK + g) % 12, :]
                        ins = mm(b[BLK * j:BLK * (j + 1), 0:P], hqT[:, h, t0 + BLK * j:t0 + BLK * (j + 1)], s0,
                                 start=False, stop=True, skip_group_check=True)
                    mark["O", h, t] = A.close(ins)

                increments(0)
                for t in range(NT):
                    if t + 1 < NT:
                        increments(t + 1)
                    outputs(t)

            for h in range(H):
                mem_kv(2 * h)
                mem_kv(2 * h + 1)
                hgrn(h)
            for half in range(2):
                for m in range(2):
                    b = A.open(pe)
                    pe.wait_ge(a_free, mark["proj", 8, 1])
                    for c in range(4):
                        k = 4 * half + c
                        ins = tr(b[:, c * P:(c + 1) * P], mkN[:, m, k * P:(k + 1) * P], ident)
                    mark["mkT"] = A.close(ins)
            for t, (t0, rows) in enumerate(TILES):
                pe.wait_ge(mix_ready, t + 1)
                b = A.open(pe)
                for c in range(4):
                    ins = tr(b[:, c * P:c * P + rows], o_da[0:rows, t, c * P:(c + 1) * P], ident[0:rows, 0:rows])
                A.close(ins)
            for h in range(H):
                pe.wait_ge(mix_ready, NT + h + 1)
                b = A.open(pe)
                for t in range(4):
                    ins = tr(b[:, t * P:(t + 1) * P], o_hg[:, t, h * P:(h + 1) * P], ident)
                A.close(ins)
                b = A.open(pe)
                ins = tr(b[:, 0:DEC], o_hg[0:DEC, SAMPLE, h * P:(h + 1) * P], ident[0:DEC, 0:DEC])
                mark["mixT"] = A.close(ins)
            pe.wait_ge(a_free, mark["mixT"])
            for t in range(NT):
                proj_N(11, actT, t, V)
            for t in range(NT):
                proj_N(12, actT, t, V)
                if t >= 1:
                    norm(7 + t - 1, hn3[(t - 1) % 2], TILES[t - 1][1])
            for half in range(2):
                for m in range(2):
                    b = A.open(pe)
                    pe.wait_ge(ldcm, 32)
                    for c in range(4):
                        k = 4 * half + c
                        ins = tr(b[:, c * P:(c + 1) * P], cmkN[:, m, k * P:(k + 1) * P], ident)
                    A.close(ins)
            def mem_scores(t):
                t0, rows = TILES[t]
                if t == 0:
                    pe.wait_ge(a_free, mark["proj", 14, 3])
                    pe.wait_ge(s_free, NT * H)
                else:
                    pe.wait_ge(a_free, mark["proj", 14, 7])
                    pe.wait_ge(mp_ready, t)
                keys = mkT if t < SAMPLE else cmkT
                for h in range(H):
                    for c in range(2):
                        o = pair[0:rows, h // 2, (h % 2) * NMEM:(h % 2 + 1) * NMEM]
                        ins = mm(o, qmT[:, 2 * h + c, t0:t0 + rows], keys[:, 2 * h + c, :], start=c == 0, stop=c == 1)
                ins.then_inc(s_full, 1)

            def mem_values(t):
                t0, rows = TILES[t]
                pe.wait_ge(mpn_ready, t + 1)
                for half in range(2):
                    b = A.open(pe)
                    for c in range(4):
                        j = 4 * half + c
                        ins = tr(b[:, c * P:c * P + rows], Pm[t % 2][0:rows, j // 2, (j % 2) * P:(j % 2 + 1) * P],
                                 ident[0:rows, 0:rows])
                    done = A.close(ins)
                pe.wait_ge(a_free, done)
                if t == SAMPLE:
                    pe.wait_ge(ldcm, 32)
                vals = mvN if t < SAMPLE else cmvN
                for half in range(2):
                    b = V.open(pe)
                    for c in range(4):
                        j = 4 * half + c
                        for m in range(2):
                            ins = mm(b[:, c * P:c * P + rows], vals[:, m, j * P:(j + 1) * P],
                                     pT[:, 2 * (j // 2) + m, 0:rows], start=m == 0, stop=m == 1)
                    mark["omT", t] = V.close(ins)

            for u in (13, 14):
                for j, (c, t0) in enumerate(T_JOBS):
                    if u == 13 and c == 0:
                        pe.wait_ge(v_free, mark["norm", 7 + (2 if t0 == 0 else SAMPLE), 1])
                    proj_T(u, hmT, j)
                    if u == 13 and j == 0:
                        norm(7 + SAMPLE, hn3[SAMPLE % 2], DEC)
                    if u == 14 and j == 5:
                        mem_scores(0)
            for t in range(NT + 2):
                if 1 <= t < NT:
                    mem_scores(t)
                if t >= 2:
                    pe.wait_ge(v_free, mark["omT", t - 2])
                    proj_N(15, actT, t - 2, V)
                if 1 <= t <= NT:
                    mem_values(t - 1)
            def router(t):
                t0, rows = TILES[t]
                if t == 0:
                    pe.wait_ge(ldrt, 48)
                pe.wait_ge(v_free, mark["norm", 12 + t, 1])
                b = V.open(pe)
                for k in range(KC):
                    ins = mm(b[0:rows, 0:36], hmT[:, k, t0:t0 + rows], rw[:, k, :], start=k == 0, stop=k == KC - 1)
                V.close(ins)

            for t in range(NT):
                proj_N(16, actT, t, V)
                if t >= 1:
                    norm(12 + t - 1, hn3[(t - 1) % 2], TILES[t - 1][1])
                if t >= 2:
                    router(t - 2)
            router(NT - 2)
            norm(12 + SAMPLE, hn3[SAMPLE % 2], DEC)
            router(SAMPLE)
            pe.wait_ge(pool_c, 2)
            pe.wait_ge(sel_ready, 1)
            b = V.open(pe)
            mm(b[:, 0:(NT + 1) * NE].rearrange("p (t e) -> p t e", e=NE), ones, before, start=True, stop=False, skip_group_check=True)
            V.close(mm(b[:, 0:NT * NE].rearrange("p (t e) -> p t e", e=NE), upper, r_sel, start=False, stop=True, skip_group_check=True))
            b = V.open(pe)
            for k in range(2):
                pe.wait_ge(hot_ready, k + 1)
                for t, (_, rows) in enumerate(TILES):
                    ins = mm(b[:, 0:NB // 2], hot_s[k][0:rows, t, :], hot_p[k][0:rows, t, :], start=k == 0 and t == 0,
                             stop=k == 1 and t == SAMPLE)
            mark["sidx"] = V.close(ins)
            pe.wait_ge(v_free, V.filled)
            pe.wait_ge(a_free, A.filled)

            def pair_of_blocks(i):
                later = not isinstance(i, int)
                pe.wait_ge(xg_ld, 16 * (i + 1))
                for k in range(KC):
                    ins = tr(pair[:, k // 4, (k % 4) * P:(k % 4 + 1) * P], xg[:, k * P:(k + 1) * P], ident)
                ins.then_inc(tx_full, 1)
                for j in range(2):
                    pe.wait_ge(ldg[j], 16 * (i + 1))
                    pe.wait_ge(ldu[j], 16 * (i + 1))
                    if j == 0:
                        pe.wait_ge(xT_cp, i + 1)
                    g, u = banks[1 + j][CAP * j:CAP * (j + 1), :], banks[1 + j][CAP * (1 - j):CAP * (2 - j), :]
                    for k in range(KC):
                        x = xgT[:, k, CAP * j:CAP * (j + 1)]
                        mm(g, x, wexp[j][0][:, k, :], start=k == 0, stop=k == KC - 1)
                        ins = mm(u, x, wexp[j][1][:, k, :], start=k == 0, stop=k == KC - 1)
                    ins.then_inc(gu_full, 1)
                pe.wait_ge(hE_ready, i + 1)
                for k in range(4):
                    ins = tr(banks[3][:, k * P:(k + 1) * P], hE[:, k * P:(k + 1) * P], ident)
                ins.then_inc(th_full, 1)
                pe.wait_ge(hT_cp, i + 1)
                if later:
                    pe.wait_ge(y_cp, 2 * i)
                for j in range(2):
                    pe.wait_ge(ldd[j], 16 * (i + 1))
                    for k in range(4):
                        for n in range(2):
                            ins = mm(banks[4 + j][CAP * n:CAP * (n + 1), :], hET[:, k, CAP * j:CAP * (j + 1)],
                                     wexp[j][2][:, k, 512 * n:512 * (n + 1)], start=k == 0, stop=k == 3)
                    ins.then_inc(dn_full, 1)

            moe_loops(pe, pair_of_blocks)

        @block.sync
        def _(sp):
            def load_unit(u):
                if u >= NSLOT:
                    s, n = unit_done[u - NSLOT]
                    sp.wait_ge(s, n)
                name, c = UNITS[u]
                src = a[name][0].rearrange("(k p) n -> p k n", p=P)[:, :, c:c + 512]
                sp.dma_start(wslot[u % NSLOT], src).then_inc(ldw[u % NSLOT], 16)

            def rows_of_x(t):
                t0, rows = TILES[t]
                return a["x_prompt"][0, t0:t0 + rows, :] if t < SAMPLE else a["x_sample"][0]

            def load_stage(n, dst, src, rows):
                sp.dma_start(dst[0:rows, :], src).then_inc(ldx[n], 16)

            for n in range(NT):
                load_stage(n, stage1[n], rows_of_x(n), TILES[n][1])
            load_unit(0)
            load_unit(1)
            sp.wait_ge(pool_c, 2)
            sp.dma_start(y_dram[NE * CAP:, :].rearrange("(c p) n -> p c n", p=P),
                         area(OZ, 1024).unsqueeze(1).broadcast_to([P, OVER * CAP // P, 1024])).then_inc(y_zero, 16)
            sp.dma_start(ckN, a["cache_diff_k"][0, 0].rearrange("t h d -> t (h d)")).then_inc(ldcache, 16)
            sp.dma_start(cvN, a["cache_diff_v"][0, 0].rearrange("t h d -> t (h d)")).then_inc(ldcache, 16)
            for u in range(2, 6):
                load_unit(u)
            sp.wait_ge(a_free, mark["proj", 3, SAMPLE])
            sp.dma_start(nk_p[0, 0].rearrange("(t p) h d -> p t (h d)", p=P), kN[:, 0:4, :]).then_inc(stk, 16)
            sp.dma_start(nk_s[0, 0].rearrange("t h d -> t (h d)"), kN[0:DEC, SAMPLE, :]).then_inc(stk, 16)
            sp.wait_ge(a_free, mark["ckT"])
            for m in range(2):
                load_stage(m, stage2[m], a["mem_prompt"][0, m * P:(m + 1) * P, :], P)
            load_unit(6)
            sp.wait_ge(a_free, mark["proj", 4, SAMPLE])
            sp.dma_start(nv_p[0, 0].rearrange("(t p) h d -> p t (h d)", p=P), vN[:, 0:4, :]).then_inc(stv, 16)
            sp.dma_start(nv_s[0, 0].rearrange("t h d -> t (h d)"), vN[0:DEC, SAMPLE, :]).then_inc(stv, 16)
            load_unit(7)
            load_unit(8)
            sp.wait_ge(w_ready, NT * H)
            sp.wait_ge(a_free, mark["o_da", SAMPLE])
            sp.wait_ge(ldcache, 32)
            sp.dma_start(St0, a["state_hgrn"][0, 0].rearrange("h d v -> d h v")).then_inc(ldcache, 16)
            load_unit(9)
            load_unit(10)
            sp.wait_ge(a_free, mark["proj", 8, 1])
            sp.dma_start(nmk[0, 0].rearrange("(m p) h d -> p m (h d)", p=P), mkN).then_inc(stmk, 16)
            sp.wait_ge(a_free, mark["proj", 10, 1])
            sp.dma_start(nmv[0, 0].rearrange("(m p) h d -> p m (h d)", p=P), mvN).then_inc(stmv, 16)
            load_unit(11)
            load_unit(12)
            sp.wait_ge(a_free, mark["mkT"])
            sp.wait_ge(stmk, 16)
            sp.dma_start(x_sb[:, 0:4, :], a["x_prompt"][0].rearrange("(t p) n -> p t n", p=P)).then_inc(ldxr, 16)
            sp.dma_start(x_sb[0:DEC, SAMPLE, :], a["x_sample"][0]).then_inc(ldxr, 16)
            sp.wait_ge(v_free, mark["G", H - 1, SAMPLE])
            sp.dma_start(ns_p[0, 0].rearrange("h d v -> d h v"), SF[:, 0:H, :]).then_inc(sts, 16)
            sp.dma_start(ns_s[0, 0].rearrange("h d v -> d h v"), SF[:, H:2 * H, :]).then_inc(sts, 16)
            load_unit(13)
            sp.wait_ge(a_free, mark["mixT"])
            sp.dma_start(cmkN, a["cache_mem_k"][0, 0].rearrange("(m p) h d -> p m (h d)", p=P)).then_inc(ldcm, 16)
            sp.dma_start(cmvN, a["cache_mem_v"][0, 0].rearrange("(m p) h d -> p m (h d)", p=P)).then_inc(ldcm, 16)
            for u in (14, 15, 16):
                load_unit(u)

            def load_part(j, which, e):
                name = ("exp_w_gate", "exp_w_up", "exp_w_down")[which]
                src = a[name][0, e:e + 1] if isinstance(e, int) else a[name][0][bass.ds(e, 1)]
                sp.dma_start(wexp[j][which], src.rearrange("o (k p) n -> p (o k) n", p=P)).then_inc((ldg, ldu, ldd)[which][j], 16)

            sp.wait_ge(v_free, mark["omT", SAMPLE])
            sp.dma_start(rw[:, :, 0:4], a["router_group_w"][0].rearrange("(k p) n -> p k n", p=P)).then_inc(ldrt, 16)
            sp.dma_start(rw[:, :, 4:36], a["router_expert_w"][0].rearrange("(k p) n -> p k n", p=P)).then_inc(ldrt, 16)
            sp.dma_start(gfin, a["final_norm_g"].rearrange("(o n) -> o n", o=1).broadcast_to([P, D])).then_inc(ldrt, 16)
            load_part(1, 0, 1)
            load_part(1, 1, 1)
            load_part(0, 2, 0)
            for n in range(NT):
                sp.wait_ge(hn_ready, 12 + n + 1)
                t0, rows = TILES[n]
                sp.dma_start(hn_dram[t0:t0 + rows, :], hn3[n % 2][0:rows, :]).then_inc(hn_st[n % 2], 16)
            s, v = unit_done[16]
            sp.wait_ge(s, v)
            for which in range(2):
                load_part(0, which, 0)
            sp.wait_ge(v_free, mark["norm", 12 + SAMPLE, 1])
            sp.wait_ge(sel_ready, 1)
            load_part(1, 2, 1)

            def load_pair(i, e):
                for j in range(2):
                    sp.wait_ge(gu_full, 2 * i + (j - 1))
                    load_part(j, 0, e[j])
                    load_part(j, 1, e[j])
                for j in range(2):
                    sp.wait_ge(dn_full, 2 * i + (j - 1))
                    load_part(j, 2, e[j])

            with sp.Fori(1, NE // 2) as i:
                load_pair(i, [2 * i, 2 * i + 1])
            sp.wait_ge(meta_ready, 1)
            pairs = sp.value_load(np_i[0:1, 0:1], min_val=0, max_val=OVER // 2)
            over = sp.value_load(over_i[0:1, 0:1], min_val=0, max_val=OVER)
            with sp.If(pairs > 0):
                with sp.Fori(NE // 2, pairs + NE // 2) as i:
                    e = [sp.value_load(meta_i[0:1, bass.ds(2 * i + (j - NE), 1)], min_val=0, max_val=NE - 1) for j in range(2)]
                    with sp.If(over > 2 * i + (1 - NE)):
                        load_pair(i, e)
                    with sp.Else():
                        sp.wait_ge(gu_full, 2 * i - 1)
                        load_part(0, 0, e[0])
                        load_part(0, 1, e[0])
                        sp.wait_ge(gu_full, 2 * i)
                        sp.sem_inc(ldg[1], 16)
                        sp.sem_inc(ldu[1], 16)
                        sp.wait_ge(dn_full, 2 * i - 1)
                        load_part(0, 2, e[0])
                        sp.wait_ge(dn_full, 2 * i)
                        sp.sem_inc(ldd[1], 16)
            for t, (t0, rows) in enumerate(TILES):
                sp.wait_ge(fin_ready, t + 1)
                dst = y_prompt[0, t0:t0 + rows, :] if t < SAMPLE else y_sample[0]
                sp.dma_start(dst, fin[t % 3][0:rows, :]).then_inc(fin_st[t % 3], 16)
            for s, n in ((stk, 32), (stv, 32), (sts, 32), (stmk, 16), (stmv, 16), (hn_st[0], 48), (hn_st[1], 32),
                         (fin_st[0], 32), (fin_st[1], 32), (fin_st[2], 16)):
                sp.wait_ge(s, n)

        @block.gpsimd
        def _(po):
            g = nc.gpsimd
            n = Chain(po, pool_s)
            n.step(g.memset(ident, 0.0))
            n.step(g.memset(neghalf, -0.5))
            n.settle()
            g.affine_select(out=ident, in_=ident, pattern=[[-1, P]], compare_op=ALU.not_equal, fill=1.0, base=0,
                            channel_multiplier=1).then_inc(pool_c, 1)
            po.wait_ge(pool_c, 1)

            def inv_std(out, total, count):
                n.link(g.tensor_scalar(out, total, 1.0 / count, EPS, ALU.mult, ALU.add))
                return g.tensor_tensor(out, out, neghalf[0:out.shape[0], :].broadcast_to(list(out.shape)), ALU.pow)

            def norm(p, rows):
                po.wait_ge(ssq_ready, p + 1)
                inv_std(rstd[0:rows, p:p + 1], ssq[0:rows, p:p + 1], D).then_inc(rstd_ready, 1)
                po.wait_ge(rstd_ready, p + 1)

            for t in range(NT):
                norm(t, TILES[t][1])
            n.step(g.memset(ones, 1.0))
            n.step(g.memset(upper, 1.0))
            n.step(g.memset(bdmask, 1))
            n.step(g.iota(dist_i, pattern=[[-1, 512]], base=SEQ - P, channel_multiplier=1))
            n.settle()
            n.step(g.affine_select(out=upper, in_=upper, pattern=[[1, P]], compare_op=ALU.is_gt, fill=0.0, base=0, channel_multiplier=-1))
            n.step(g.affine_select(out=bdmask, in_=bdmask, pattern=[[1, P]], compare_op=ALU.is_ge, fill=0, base=0, channel_multiplier=-1))
            n.settle()
            bd3 = bdmask.rearrange("p (j c) -> p j c", j=4)
            n.step(g.affine_select(out=bd3, in_=bd3, pattern=[[-BLK, 4], [0, BLK]], compare_op=ALU.is_ge, fill=0, base=0, channel_multiplier=1))
            n.step(g.iota(iota_i, pattern=[[1, 2 * CAP]], base=0, channel_multiplier=0))
            n.step(g.iota(tok_i, pattern=[[P, NT]], base=0, channel_multiplier=1))
            n.step(g.memset(PT, 0.0))
            n.step(g.memset(Vbd, 0.0))
            n.settle()
            g.memset(gss, 1.0).then_inc(pool_c, 1)
            po.wait_ge(pool_c, 2)
            po.wait_ge(cst, 1)

            def spread_v(h):
                if h == 0:
                    po.wait_ge(y_zero, 16)
                    po.wait_ge(a_free, mark["proj", 5, SAMPLE])
                else:
                    po.wait_ge(v_full, mark["G", h - 1, SAMPLE])
                for j in range(4):
                    nt = NT if j < DEC // BLK else NT - 1
                    s = slice(BLK * j, BLK * (j + 1))
                    ins = g.tensor_copy(Vbd[s, 0:nt, j, :], hiN[s, 0:nt, h * P:(h + 1) * P])
                    if j < 3:
                        n.link(ins)
                ins.then_inc(vbd_ready, 1)
                po.wait_ge(vbd_ready, h + 1)

            for t in range(NT):
                rows = TILES[t][1]
                v3 = o_da[0:rows, t, :].rearrange("p (h d) -> p h d", h=H)
                po.wait_ge(a_free, mark["o_da", t])
                n.link(inv_std(hrs[0:rows, t, :], hss[0:rows, t, :], P))
                n.link(g.tensor_tensor(v3, v3, hrs[0:rows, t, :].unsqueeze(2).broadcast_to([rows, H, P]), ALU.mult))
                g.tensor_tensor(v3, v3, gsub[0:rows, :].unsqueeze(1).broadcast_to([rows, H, P]), ALU.mult).then_inc(mix_ready, 1)
                po.wait_ge(mix_ready, t + 1)
                if t == NT - 3:
                    spread_v(0)
                    po.wait_ge(ssq_ready, NT + 2)
                    for m in range(2):
                        norm(NT + m, P)

            def gated_head(h):
                c = slice(h * P, (h + 1) * P)
                po.wait_ge(a_free, mark["O", h, SAMPLE])
                n.link(inv_std(grs[:, h, :], gss[:, h, :], P))
                if h == 0:
                    po.wait_ge(sg_ready, NT)
                n.link(g.tensor_tensor(o_hg[:, 0:4, c], o_hg[:, 0:4, c], grs[:, h, 0:4].unsqueeze(2).broadcast_to([P, 4, P]), ALU.mult))
                n.link(g.tensor_tensor(o_hg[0:DEC, SAMPLE, c], o_hg[0:DEC, SAMPLE, c],
                                       grs[0:DEC, h, SAMPLE:NT].broadcast_to([DEC, P]), ALU.mult))
                n.link(g.tensor_tensor(o_hg[:, 0:4, c], o_hg[:, 0:4, c], hgN[:, 0:4, c], ALU.mult))
                g.tensor_tensor(o_hg[0:DEC, SAMPLE, c], o_hg[0:DEC, SAMPLE, c], hgN[0:DEC, SAMPLE, c], ALU.mult).then_inc(mix_ready, 1)
                po.wait_ge(mix_ready, NT + h + 1)

            for h in range(1, H):
                spread_v(h)
                gated_head(h - 1)
            gated_head(H - 1)
            for p0 in (7, 12):
                for t in range(NT):
                    norm(p0 + t, TILES[t][1])
            po.wait_ge(slot_ready, 1)
            po.wait_ge(v_free, mark["sidx"])
            po.wait_ge(hn_st[0], 48)
            po.wait_ge(hn_st[1], 32)
            n.link(g.memset(gdum, 0))

            def pair_of_blocks(i):
                if not isinstance(i, int):
                    po.wait_ge(tx_full, i)
                g.tensor_copy(gidx, sidx[:, bass.ds(i, 1)]).then_inc(gi_ready, 1)
                po.wait_ge(gi_ready, i + 1)
                g.tensor_tensor(gdum[:, 0:1], gdum[:, 1:2], gdum[:, 2:3], ALU.add)
                g.indirect_dma_start(out=xg, out_offset=None, in_=hn_dram,
                                     in_offset=bass.IndirectOffsetOnAxis(ap=gidx, axis=0)).then_inc(xg_ld, 16)

            moe_loops(po, pair_of_blocks)
            po.wait_ge(y_all, 1)
            for t, (_, rows) in enumerate(TILES):
                for k in range(2):
                    g.indirect_dma_start(out=yg[t][k][0:rows, :], out_offset=None, in_=y_dram,
                                         in_offset=bass.IndirectOffsetOnAxis(ap=slot_i[0:rows, k, t:t + 1], axis=0)).then_inc(yg_ld[t], 16)
            for t, (_, rows) in enumerate(TILES):
                po.wait_ge(fssq, t + 1)
                inv_std(rstd[0:rows, 17 + t:18 + t], ssq[0:rows, 17 + t:18 + t], D).then_inc(frstd, 1)
                po.wait_ge(frstd, t + 1)

        @block.scalar
        def _(act):
            f = nc.scalar.activation
            n = Chain(act, ac)

            def row(ap, width, parts=P):
                return ap.rearrange("(o n) -> o n", o=1).broadcast_to([parts, width])

            for i, name in enumerate(("ln_mix_g", "mem_norm_g", "ln_mem_g", "ln_ffn_g")):
                act.dma_start(gains[:, i, :], a[name][0].rearrange("(k p) -> p k", p=P),
                              allow_slow_non_contiguous=True).then_inc(ldc if i else ldgain, 16)
            act.dma_start(gsub, row(a["da_subln_g"][0], P)).then_inc(ldc, 16)
            act.dma_start(ggn, row(a["hg_gnorm_g"][0], P)).then_inc(ldc, 16)
            act.dma_start(lamp, row(a["da_lambda"][0].rearrange("f d -> (f d)"), 256)).then_inc(ldc, 16)
            act.dma_start(lbl, a["hg_lb_logits"].rearrange("l (h p) -> p l h", p=P),
                          allow_slow_non_contiguous=True).then_inc(ldc, 16)
            act.dma_start(rbias[:, 0:GROUPS], row(a["router_group_b"][0], GROUPS)).then_inc(ldc, 16)
            act.dma_start(rbias[:, GROUPS:], row(a["router_expert_b"][0], NE)).then_inc(ldc, 16)

            def drain(dst, get):
                b = A.take(act)
                A.done(f(dst, get(b), ACT.Copy))

            def quads(rows):
                return lambda b: b[:, :].rearrange("p (c t) -> p c t", c=4)[:, :, 0:rows]

            def drain_T(dst):
                for j in range(len(T_JOBS)):
                    drain_T1(dst, j)

            def drain_T1(dst, j):
                c, t0 = T_JOBS[j]
                drain(dst[:, c, t0:t0 + HALF], lambda b: b[:, 0:HALF])

            def drain_N(dst, t):
                if t < SAMPLE:
                    drain(dst[:, t, :], lambda b: b[:, :])
                else:
                    b = A.take(act)
                    n.step(f(dst[0:DEC, t, 0:256], b[0:DEC, 0:256], ACT.Copy))
                    A.done(f(dst[0:DEC, t, 256:512], b[DEC:2 * DEC, 0:256], ACT.Copy))

            act.wait_ge(c_in, 1)
            f(lbl, lbl, ACT.Exp).then_inc(c_exp, 1)
            f(lam[:, 0:2], lam[:, 0:2], ACT.Exp).then_inc(c_exp, 1)
            def hgrn_exp(h):
                f(hfT[:, h, :], hfT[:, h, :], ACT.Exp, scale=-1.0).then_inc(pre_act, 1)
                f(gQ, hqT[:, h, :], ACT.Exp, scale=-1.0).then_inc(pre_act, 1)

            def hgrn_log(h):
                act.wait_ge(pre_dve, 3 * h + 1)
                f(qHat[h], gS, ACT.Ln, bias=lb[:, h:h + 1], scale=oml[:, h:h + 1]).then_inc(pre_act, 1)

            def hgrn_decays(h):
                act.wait_ge(pre_dve, 3 * h + 2)
                f(qHat[h], kHat[h], ACT.Exp).then_inc(pre_act, 1)
                f(EB[:, h, :], gB.rearrange("p (b c) -> p b c", c=BLK)[:, :, BLK - 1], ACT.Exp).then_inc(pre_act, 1)
                act.wait_ge(pre_act, 8 * h + 5)
                f(kHat[h], kHat[h], ACT.Exp, scale=-1.0).then_inc(pre_act, 1)
                f(gB, gB, ACT.Exp).then_inc(pre_act, 1)
                f(gE, gE, ACT.Exp).then_inc(pre_act, 1)

            drain_T(hfT)
            drain_T(hqT)
            act.wait_ge(a_free, mark["proj", 1, 7])
            for h in range(H):
                hgrn_exp(h)
                if h < 2:
                    drain_T1(qT, 4 * h)
                    drain_T1(qT, 4 * h + 1)
                else:
                    for t in ((0,), (3, SAMPLE))[h - 2]:
                        drain_N(kN, t)
                hgrn_log(h)
                if h < 2:
                    drain_T1(qT, 4 * h + 2)
                elif h == 2:
                    drain_N(kN, 1)
                else:
                    for t, (t0, rows) in enumerate(TILES):
                        drain(kT[:, :, t0:t0 + rows], quads(rows))
                    drain(ckT, quads(P))
                hgrn_decays(h)
                if h < 2:
                    drain_T1(qT, 4 * h + 3)
                if h == 2:
                    drain_N(kN, 2)

            drains = []

            def drain_head(dst, t, h, total):
                rows = TILES[t][1]
                b = A.take(act)
                n.step(f(dst[0:rows, t, h * P:(h + 1) * P], b[0:rows, 0:P], ACT.Copy))
                k = len(drains) % 4
                if len(drains) >= 4:
                    act.wait_ge(a_free, drains[-4])
                A.done(f(sq[0:rows, k * P:(k + 1) * P], b[0:rows, 0:P], ACT.Square, accum_out=total))
                drains.append(A.drained)

            def exps(i):
                t, h = divmod(i, H)
                rows = TILES[t][1]
                keys = (t + 1) * P if t < SAMPLE else PAST + DEC
                act.wait_ge(nb_ready, i + 1)
                for c in range(2):
                    u = U[i % 3][0:rows, c, 0:keys]
                    ins = f(u, u, ACT.Exp, bias=nb[0:rows, i % 2, c:c + 1], scale=DA_SCALE,
                            accum_out=rs[0:rows, i % 2, c:c + 1])
                ins.then_inc(p_ready, 1)

            def exp_gate(t):
                rows = TILES[t][1]
                if t == 0:
                    act.wait_ge(a_free, mark["proj", 6, SAMPLE])
                f(eHG[t][0:rows, :], hgN[0:rows, t, :], ACT.Exp, scale=-1.0).then_inc(eg_ready, 1)

            for i in range(NT * H + 3):
                if i < NT * H:
                    exps(i)
                if i in FILL:
                    drain_N((vN, hiN, hgN)[FILL[i][0] - 4], FILL[i][1])
                if 2 <= i <= NT * H + 1:
                    t = (i - 2) // H
                    rows = TILES[t][1]
                    dst = wT[i % 2]
                    if t < SAMPLE:
                        drain(dst[:, 0:t + 1, :], lambda b: b[:, 0:(t + 1) * P].rearrange("p (j q) -> p j q", q=P))
                    else:
                        b = A.take(act)
                        n.step(f(dst[:, 0, 0:rows], b[:, 0:rows], ACT.Copy))
                        A.done(f(dst[0:DEC, 1, 0:rows], b[0:DEC, P:P + rows], ACT.Copy))
                if i == 3:
                    act.wait_ge(stk, 32)
                if i >= 3:
                    t, h = divmod(i - 3, H)
                    drain_head(o_da, t, h, hss[0:TILES[t][1], t, h:h + 1])
                if i >= NT * H - 1:
                    exp_gate(i - (NT * H - 1))
            exp_gate(SAMPLE)

            def hgrn_main(h):
                for j in (2 * h, 2 * h + 1):
                    dst = mkN if j < 4 else mvN
                    c = 512 * ((j // 2) % 2)
                    drain(dst[:, j % 2, c:c + 512], lambda b: b[:, :])
                drain(Kt[:, 0:4, :], quads(P))
                drain(Kt[0:DEC, SAMPLE, :], lambda b: b[0:DEC, 0:P])
                for t in range(NT):
                    drain_head(o_hg, t, h, gss[0:TILES[t][1], h, t:t + 1])

            for h in range(H):
                hgrn_main(h)
            for half in range(2):
                for m in range(2):
                    drain(mkT[:, 4 * half:4 * half + 4, m * P:(m + 1) * P], quads(P))
            for t, (t0, rows) in enumerate(TILES):
                drain(actT[:, 0:4, t0:t0 + rows], quads(rows))
            for h in range(H):
                drain(actT[:, 4 + h, 0:SEQ], lambda b: b[:, :])
                drain(actT[:, 4 + h, SEQ:TOK], lambda b: b[:, 0:DEC])
            act.wait_ge(sts, 32)
            for half in range(2):
                for m in range(2):
                    drain(cmkT[:, 4 * half:4 * half + 4, m * P:(m + 1) * P], quads(P))

            def mem_exps(t):
                rows = TILES[t][1]
                act.wait_ge(mnb_ready, t + 1)
                for h in range(H):
                    ins = f(Pm[t % 2][0:rows, h, :], pair[0:rows, h // 2, (h % 2) * NMEM:(h % 2 + 1) * NMEM], ACT.Exp,
                            bias=nb[0:rows, t % 2, h:h + 1], scale=MEM_SCALE, accum_out=rs[0:rows, t % 2, h:h + 1])
                ins.then_inc(mp_ready, 1)

            for u in range(2):
                for j in range(len(T_JOBS)):
                    drain_T1(qmT[:, 4 * u:4 * u + 4, :], j)
                    if u == 1 and j == 5:
                        mem_exps(0)
            for t in range(1, NT + 1):
                if t < NT:
                    mem_exps(t)
                rows = TILES[t - 1][1]
                for half in range(2):
                    drain(pT[:, 4 * half:4 * half + 4, 0:rows], quads(rows))
            act.wait_ge(r_need, 1)
            f(r_i4, r_t4, ACT.Exp).then_inc(r_exp, 1)
            act.wait_ge(r_need, 2)
            f(r_i, r_i, ACT.Exp).then_inc(r_exp, 1)

            def pair_of_blocks(i):
                for j in range(2):
                    act.wait_ge(gu_full, 2 * i + j + 1)
                    own, other = slice(CAP * j, CAP * (j + 1)), slice(CAP * (1 - j), CAP * (2 - j))
                    f(eG[own, :], banks[1 + j][own, :], ACT.Exp, scale=-1.0)
                    f(eU[own, :], banks[1 + j][other, :], ACT.Copy).then_inc(act_u, 1)
                for j in range(2):
                    act.wait_ge(dn_full, 2 * i + j + 1)
                    if not isinstance(i, int):
                        act.wait_ge(y_st[j], 32 * i)
                    f(yS[j], banks[4 + j][:, :], ACT.Copy).then_inc(y_cp, 1)
                    act.wait_ge(y_cp, 2 * i + j + 1)
                    for half in range(2):
                        act.dma_start(y_dram[bass.ds((2 * i + j) * CAP, CAP), 512 * half:512 * (half + 1)],
                                      yS[j][CAP * half:CAP * (half + 1), :]).then_inc(y_st[j], 16)

            pairs = moe_loops(act, pair_of_blocks)
            for j in range(2):
                act.wait_ge(y_st[j], 32 * (pairs + NE // 2))
            act.sem_inc(y_all, 1)
            for t, (_, rows) in enumerate(TILES):
                act.wait_ge(fsum, t + 1)
                f(yg[t][0][0:rows, :], fin[t % 3][0:rows, :], ACT.Square, accum_out=ssq[0:rows, 17 + t:18 + t]).then_inc(fssq, 1)

        @block.vector
        def _(ve):
            v = nc.vector
            n = Chain(ve, dv)
            ts, tt, stt, red = v.tensor_scalar, v.tensor_tensor, v.scalar_tensor_tensor, v.tensor_reduce

            def sum_squares(p, src, hn, rows):
                v.tensor_tensor_reduce(hn[0:rows, :], src, src, 1.0, 0.0, ALU.mult, ALU.add,
                                       ssq[0:rows, p:p + 1]).then_inc(ssq_ready, 1)

            def norm_rows(p, src, hn, rows):
                ve.wait_ge(rstd_ready, p + 1)
                ts(hn[0:rows, :], src, rstd[0:rows, p:p + 1], None, ALU.mult).then_inc(hn_ready, 1)

            def drain_norm(dst, kind, t0, rows):
                for half in range(2):
                    b = V.take(ve)
                    k = slice(4 * half, 4 * half + 4)
                    V.done(tt(dst[:, k, t0:t0 + rows], b[:, :].rearrange("p (c t) -> p c t", c=4)[:, :, 0:rows],
                              gains[:, kind, k].unsqueeze(2).broadcast_to([P, 4, rows]), ALU.mult))

            for p in range(NT + 1):
                if p < NT:
                    rows = TILES[p][1]
                    ve.wait_ge(ldx[p], 16)
                    if p:
                        ve.wait_ge(ssq_ready, p)
                    sum_squares(p, stage1[p][0:rows, :], squares, rows)
                if p >= 1:
                    if p >= 3:
                        if p == 3:
                            ve.wait_ge(ldgain, 16)
                        drain_norm(actT, 0, *TILES[p - 3])
                    norm_rows(p - 1, stage1[p - 1][0:TILES[p - 1][1], :], hn1[(p - 1) % 2], TILES[p - 1][1])
            for p in range(NT - 2, NT):
                drain_norm(actT, 0, *TILES[p])
            ve.wait_ge(pool_c, 2)
            n.step(v.tensor_copy(tokf, tok_i))
            ve.wait_ge(ldc, 16 * NCONST)
            lp = lamp.rearrange("p (f d) -> p f d", f=4)
            for i in range(2):
                n.step(tt(lamt[:, i, :], lp[:, 2 * i, :], lp[:, 2 * i + 1, :], ALU.mult))
            n.step(tt(lb, lbl[:, 0, :], lbl[:, 1, :], ALU.max))
            n.settle()
            n.step(red(lam[:, 0:2], lamt, AX_X, ALU.add))
            tt(lbl, lbl, lb.unsqueeze(1).broadcast_to([P, 2, H]), ALU.subtract).then_inc(c_in, 1)
            ve.wait_ge(c_exp, 2)
            n.link(tt(oml, lbl[:, 0, :], lbl[:, 1, :], ALU.add))
            n.link(v.reciprocal(oml, oml))
            n.link(tt(lb, lbl[:, 0, :], oml, ALU.mult))
            n.step(ts(oml, lb, -1.0, 1.0, ALU.mult, ALU.add))
            n.link(tt(lam[:, 2:3], lam[:, 1:2], lam[:, 0:1], ALU.subtract))
            n.step(ts(lam[:, 2:3], lam[:, 2:3], -LAM_INIT, None, ALU.add))
            ts(gsub, gsub, 1.0 - LAM_INIT, None, ALU.mult).then_inc(cst, 1)
            ve.wait_ge(cst, 1)


            def hgrn_pre(h):
                def blocks(x):
                    return x.rearrange("p (b c) -> p b c", c=BLK)
                F, Q = hfT[:, h, :], hqT[:, h, :]
                k = oml[:, h:h + 1]
                ve.wait_ge(pre_act, 8 * h + 1)
                n.link(ts(gS, F, BIG, 1.0, ALU.min, ALU.add))
                v.reciprocal(gS, gS).then_inc(pre_dve, 1)
                ve.wait_ge(pre_dve, 3 * h + 1)
                n.step(stt(out=F, in0=F, scalar=BIG, in1=gS, op0=ALU.min, op1=ALU.mult))
                ve.wait_ge(pre_act, 8 * h + 2)
                n.link(ts(gQ, gQ, 1.0, None, ALU.add))
                n.link(v.reciprocal(gQ, gQ))
                n.step(tt(Q, Q, gQ, ALU.mult))
                ve.wait_ge(pre_act, 8 * h + 3)
                n.link(v.tensor_tensor_scan(gB, scanm, qHat[h], 0.0, ALU.mult, ALU.add))
                b3 = blocks(gB)
                mid = b3[:, :, BLK // 2 - 1:BLK // 2].broadcast_to([P, NBLK, BLK])
                end = b3[:, :, BLK - 1:BLK].broadcast_to([P, NBLK, BLK])
                n.step(tt(blocks(kHat[h]), b3, mid, ALU.subtract))
                tt(blocks(gE), end, b3, ALU.subtract).then_inc(pre_dve, 1)
                ve.wait_ge(pre_act, 8 * h + 8)
                n.settle()
                n.step(tt(qHat[h], qHat[h], Q, ALU.mult))
                n.step(stt(out=kHat[h], in0=F, scalar=k, in1=kHat[h], op0=ALU.mult, op1=ALU.mult))
                n.settle()
                n.step(tt(Q, Q, gB, ALU.mult))
                stt(out=F, in0=F, scalar=k, in1=gE, op0=ALU.mult, op1=ALU.mult).then_inc(pre_dve, 1)

            def swish_gate(t):
                rows = TILES[t][1]
                e, g = eHG[t][0:rows, :], hgN[0:rows, t, :]
                ve.wait_ge(eg_ready, t + 1)
                n.link(ts(e, e, 1.0, None, ALU.add))
                n.link(v.reciprocal(e, e))
                n.link(tt(g, g, e, ALU.mult))
                g3 = g.rearrange("p (h d) -> p h d", h=H)
                tt(g3, g3, ggn[0:rows, :].unsqueeze(1).broadcast_to([rows, H, P]), ALU.mult).then_inc(sg_ready, 1)

            n.link(v.memset(scanm, 1.0))
            n.link(v.memset(scanm.rearrange("p (b c) -> p b c", c=BLK)[:, :, 0:1], 0.0))
            for h in range(H):
                hgrn_pre(h)
            n.link(v.tensor_copy(dist, dist_i))
            n.link(stt(out=dist, in0=dist, scalar=-1.0, in1=dist, op0=ALU.mult, op1=ALU.max))
            n.step(v.memset(dist[0:64, 448:512], BIG))
            n.settle()

            def soft(i):
                t, h = divmod(i, H)
                rows = TILES[t][1]
                keys, c0 = ((t + 1) * P, SEQ - (t + 1) * P) if t < SAMPLE else (PAST + DEC, 256)
                u = U[i % 3][0:rows, :, 0:keys]
                ve.wait_ge(s_full, i + 1)
                stt(out=u, in0=dist[0:rows, c0:c0 + keys].unsqueeze(1).broadcast_to([rows, 2, keys]), scalar=-SLOPES[h] / DA_SCALE,
                    in1=pair[0:rows, :, 0:keys], op0=ALU.mult, op1=ALU.add).then_inc(s_free, 1)
                ve.wait_ge(s_free, i + 1)
                n.link(red(mx[0:rows, i % 2, 0:2], u, AX_X, ALU.max))
                ts(nb[0:rows, i % 2, 0:2], mx[0:rows, i % 2, 0:2], -DA_SCALE, None, ALU.mult).then_inc(nb_ready, 1)

            def difference(i):
                t, h = divmod(i, H)
                rows = TILES[t][1]
                keys = (t + 1) * P if t < SAMPLE else PAST + DEC
                u = U[i % 3]
                r = rc[0:rows, i % 2, :]
                ve.wait_ge(p_ready, i + 1)
                n.link(v.reciprocal(r[:, 0:2], rs[0:rows, i % 2, 0:2]))
                n.link(tt(r[:, 2:3], r[:, 1:2], lam[0:rows, 2:3], ALU.mult))
                n.link(ts(u[0:rows, 1, 0:keys], u[0:rows, 1, 0:keys], r[:, 2:3], None, ALU.mult))
                stt(out=u[0:rows, 0, 0:keys], in0=u[0:rows, 0, 0:keys], scalar=r[:, 0:1], in1=u[0:rows, 1, 0:keys],
                    op0=ALU.mult, op1=ALU.add).then_inc(w_ready, 1)

            soft(0)
            for i in range(NT * H):
                if i + 1 < NT * H:
                    soft(i + 1)
                difference(i)
                if i == NT * H - 6:
                    for m in range(2):
                        ve.wait_ge(ldx[m], 32)
                    sum_squares(NT + 1, stage2[1], hn2[0], P)
                    ve.wait_ge(ssq_ready, NT + 1)
                    sum_squares(NT, stage2[0], hn2[0], P)
                if i == NT * H - 4:
                    for m in range(2):
                        norm_rows(NT + m, stage2[m], hn2[m], P)
            swish_gate(0)
            ve.wait_ge(stv, 32)
            drain_norm(mnT, 1, 0, P)
            drain_norm(mnT, 1, P, P)
            swish_gate(1)

            def hgrn_main(h):
                b = V.take(ve)
                V.done(v.copy_predicated(PT[:, 0:4, :], bdmask.unsqueeze(1).broadcast_to([P, 4, P]),
                                         b[:, :].rearrange("p (t c) -> p t c", t=4)))
                b = V.take(ve)
                V.done(v.copy_predicated(PT[0:DEC, SAMPLE, 0:DEC], bdmask[0:DEC, 0:DEC], b[0:DEC, 0:DEC]))

                def state(g):
                    if g == SEQ // BLK:
                        return St0[:, h, :]
                    return Sring[:, (h * NBLK + g) % 12, :]

                def update(t):
                    b = V.take(ve)
                    last = TILES[t][1] // BLK - 1
                    for j in range(last + 1):
                        g = 4 * t + j
                        inc = b[:, j * P:(j + 1) * P]
                        dst = SF[:, h, :] if g == SEQ // BLK - 1 else SF[:, H + h, :] if g == NBLK - 1 else state(g + 1)
                        if g == 0:
                            ins = v.tensor_copy(dst, inc)
                        else:
                            if g == SEQ // BLK:
                                ve.wait_ge(ldcache, 48)
                            ins = stt(out=dst, in0=state(g), scalar=EB[:, h, g:g + 1], in1=inc, op0=ALU.mult, op1=ALU.add)
                        if j < last:
                            n.link(ins)
                    V.done(ins)
                    ve.wait_ge(v_free, V.drained)

                update(0)
                for t in range(1, NT):
                    update(t)

            for h in range(H):
                hgrn_main(h)
                if h == 0:
                    for t in range(2, NT):
                        swish_gate(t)

            def add(t, half):
                b = V.take(ve)
                if t < SAMPLE:
                    x = x_sb[:, t, 512 * half:512 * (half + 1)]
                    V.done(tt(x, x, b[:, :], ALU.add))
                else:
                    for part in range(2):
                        x = x_sb[0:DEC, t, 512 * half + 256 * part:512 * half + 256 * (part + 1)]
                        ins = tt(x, x, b[DEC * part:DEC * (part + 1), 0:256], ALU.add)
                        if part == 0:
                            n.step(ins)
                    V.done(ins)

            def add_rows(p0, kind, dst, stored, routed=False):
                for t, (t0, rows) in enumerate(TILES):
                    add(t, 1)
                    ve.wait_ge(v_free, V.drained)
                    n.settle()
                    if stored and t >= 2:
                        ve.wait_ge(hn_st[t % 2], 16 * (t // 2))
                    sum_squares(p0 + t, x_sb[0:rows, t, :], hn3[t % 2], rows)
                    if t:
                        drain_norm(dst, kind, *TILES[t - 1])
                    norm_rows(p0 + t, x_sb[0:rows, t, :], hn3[t % 2], rows)
                    if routed and t >= 2:
                        router_logits(t - 2)
                if routed:
                    router_logits(NT - 2)
                drain_norm(dst, kind, *TILES[SAMPLE])
                if routed:
                    router_logits(SAMPLE)

            ve.wait_ge(ldxr, 32)
            for t in range(NT):
                add(t, 0)
            add_rows(7, 2, hmT, False)
            for t in range(NT + 2):
                if t < NT:
                    rows = TILES[t][1]
                    m, q = mx[0:rows, t % 2, :], rc[0:rows, t % 2, :]
                    ve.wait_ge(s_full, NT * H + t + 1)
                    n.link(red(m, pair[0:rows].rearrange("p b (q m) -> p (b q) m", q=2), AX_X, ALU.max))
                    ts(nb[0:rows, t % 2, :], m, -MEM_SCALE, None, ALU.mult).then_inc(mnb_ready, 1)
                    ve.wait_ge(mp_ready, t + 1)
                    n.link(v.reciprocal(q, rs[0:rows, t % 2, :]))
                    pm = Pm[t % 2][0:rows, :, :]
                    tt(pm, pm, q.unsqueeze(2).broadcast_to([rows, H, NMEM]), ALU.mult).then_inc(mpn_ready, 1)
                if t >= 2:
                    add(t - 2, 0)
                if 1 <= t <= NT:
                    t0, rows = TILES[t - 1]
                    for half in range(2):
                        b = V.take(ve)
                        V.done(v.tensor_copy(actT[:, 4 * half:4 * half + 4, t0:t0 + rows],
                                             b[:, :].rearrange("p (c t) -> p c t", c=4)[:, :, 0:rows]))

            def router_logits(t):
                rows = TILES[t][1]
                b = V.take(ve)
                V.done(tt(lg[0:rows, t, :], b[0:rows, 0:36], rbias[0:rows, :], ALU.add))

            n.step(v.memset(lg, 0.0))
            n.step(v.tensor_copy(iota32, iota_i[:, 0:NE]))
            n.step(v.tensor_copy(iota_s, iota_i))
            n.step(v.memset(ones32, 1.0))
            n.step(v.memset(ovf, 0.0))
            n.step(v.memset(before[:, 0, :], 0.0))
            n.settle()
            n.link(ts(e64, iota32, float(CAP), None, ALU.mult))
            add_rows(12, 3, hmT, True, True)

            def wide(x, w):
                return x.unsqueeze(2).broadcast_to([P, NT, w])

            def over_tiles(x, w):
                return x.unsqueeze(1).broadcast_to([P, NT, w])

            ve.wait_ge(v_free, V.drained)
            n.settle()
            glog = lg[:, :, 0:GROUPS]
            n.link(red(r_g1, glog, AX_X, ALU.max))
            tt(r_t4, glog, wide(r_g1, GROUPS), ALU.subtract).then_inc(r_need, 1)
            ve.wait_ge(r_exp, 1)
            n.step(red(r_sum, r_i4, AX_X, ALU.add))
            n.settle()
            n.step(v.reciprocal(r_sum, r_sum))

            def first_best(hot, x, best, work, width, io):
                n.link(tt(work, x, wide(best, width), ALU.is_equal))
                n.link(stt(out=work, in0=work, scalar=-1000.0, in1=over_tiles(io, width), op0=ALU.mult, op1=ALU.add))
                n.link(red(r_i, work, AX_X, ALU.min))
                n.link(tt(hot, work, wide(r_i, width), ALU.is_equal))

            first_best(r_i4, glog, r_g1, r_t4, GROUPS, iota32[:, 0:GROUPS])
            n.link(ts(r_i4, r_i4, -1.0, BIG, ALU.add, ALU.mult))
            for g in range(GROUPS):
                s = slice(g * PER_GROUP, (g + 1) * PER_GROUP)
                n.step(tt(r_e[:, :, s], lg[:, :, GROUPS + g * PER_GROUP:GROUPS + (g + 1) * PER_GROUP],
                          r_i4[:, :, g:g + 1].broadcast_to([P, NT, PER_GROUP]), ALU.add))
            n.settle()
            for k in range(2):
                n.link(red(r_v[k], r_e, AX_X, ALU.max))
                first_best(r_oh[k], r_e, r_v[k], r_t, NE, iota32)
                if k == 0:
                    n.link(stt(out=r_e, in0=r_oh[0], scalar=-2.0 * BIG, in1=r_e, op0=ALU.mult, op1=ALU.add))
            n.link(tt(r_sel, r_oh[0], r_oh[1], ALU.add))
            n.step(v.memset(r_sel[DEC:P, SAMPLE, :], 0.0))
            for t in range(NT - 1):
                n.link(tt(before[:, t + 1, :], before[:, t, :], r_sel[:, t, :], ALU.add))
            tt(before[:, NT, :], before[:, SAMPLE, :], r_sel[:, SAMPLE, :], ALU.add).then_inc(sel_ready, 1)
            n.step(tt(r_i, r_v[1], r_v[0], ALU.subtract))
            v.memset(gate[0], 0.0).then_inc(r_need, 1)
            ve.wait_ge(r_exp, 2)
            n.settle()
            n.link(ts(gate[1], r_i, 1.0, None, ALU.add))
            n.link(v.reciprocal(gate[1], gate[1]))
            n.link(tt(gate[0], gate[1], r_sum, ALU.mult))
            n.link(tt(gate[1], gate[0], r_i, ALU.mult))
            b = V.take(ve)
            V.done(v.tensor_copy(rank_cnt, b[:, 0:(NT + 1) * NE]))
            ve.wait_ge(v_free, V.drained)
            n.step(ts(cnt_i, cnt, float(CAP - 1), None, ALU.add))
            n.step(tt(place, rank, over_tiles(e64, NE), ALU.add))
            n.settle()
            n.link(ts(cnt_i, cnt_i, CAP.bit_length() - 1, None, ALU.arith_shift_right))
            n.link(ts(ovf, cnt_i, -1.0, 0.0, ALU.add, ALU.max))
            n.link(v.tensor_tensor_scan(cum, ones32, ovf, 0.0, ALU.mult, ALU.add))
            n.link(tt(base, cum, ovf, ALU.subtract))
            n.link(ts(base, base, float(CAP), float(CAP * (NE - 1)), ALU.mult, ALU.add))
            n.link(tt(base, base, e64, ALU.subtract))
            n.link(stt(out=r_t, in0=rank, scalar=float(CAP), in1=over_tiles(base, NE), op0=ALU.is_ge, op1=ALU.mult))
            n.link(tt(place, place, r_t, ALU.add))
            for k in range(2):
                n.step(tt(r_hit[:, k], r_oh[k], place, ALU.mult))
            n.settle()
            n.link(red(slotf, r_hit, AX_X, ALU.add))
            v.tensor_copy(slot_i, slotf).then_inc(slot_ready, 1)
            ve.wait_ge(slot_ready, 1)
            n.step(ts(lo_i, slot_i, 2 * CAP - 1, None, ALU.bitwise_and))
            n.step(ts(hi_i, slot_i, 7, None, ALU.arith_shift_right))
            n.settle()
            n.step(v.tensor_copy(lo_f, lo_i))
            n.step(v.tensor_copy(hi_f, hi_i))
            n.settle()
            for k in range(2):
                n.step(tt(hot_s[k], over_tiles(iota_s, 2 * CAP), wide(lo_f[:, k, :], 2 * CAP), ALU.is_equal))
                n.link(tt(hot_p[k], over_tiles(iota_s[:, 0:NB // 2], NB // 2), wide(hi_f[:, k, :], NB // 2), ALU.is_equal))
                tt(hot_p[k], hot_p[k], wide(tokf, NB // 2), ALU.mult).then_inc(hot_ready, 1)
            b = V.take(ve)
            V.done(v.tensor_copy(sidx, b[:, 0:NB // 2]))
            n.step(tt(cmp_e, cum.unsqueeze(1).broadcast_to([P, OVER, NE]),
                      iota32[:, 0:OVER].unsqueeze(2).broadcast_to([P, OVER, NE]), ALU.is_le))
            n.step(ts(cmp_p[:, 0:OVER // 2], iota32[:, 0:OVER:2], cum[:, NE - 1:NE], None, ALU.is_lt))
            n.settle()
            n.step(red(eo, cmp_e, AX_X, ALU.add))
            n.step(red(npf, cmp_p[:, 0:OVER // 2], AX_X, ALU.add))
            n.settle()
            n.link(ts(eo, eo, float(NE - 1), None, ALU.min))
            n.step(v.tensor_copy(meta_i, eo))
            n.step(v.tensor_copy(over_i, cum[:, NE - 1:NE]))
            n.settle()
            v.tensor_copy(np_i, npf).then_inc(meta_ready, 1)

            def pair_of_blocks(i):
                ve.wait_ge(tx_full, i + 1)
                for half in range(2):
                    k = slice(4 * half, 4 * half + 4)
                    ins = tt(xgT[:, k, :], pair[:, half, :].rearrange("p (k t) -> p k t", k=4),
                             gains[:, 3, k].unsqueeze(2).broadcast_to([P, 4, P]), ALU.mult)
                ins.then_inc(xT_cp, 1)
                for j in range(2):
                    own = slice(CAP * j, CAP * (j + 1))
                    ve.wait_ge(act_u, 2 * i + j + 1)
                    tt(eU[own, :], banks[1 + j][own, :], eU[own, :], ALU.mult).then_inc(mdv, 1)
                ts(eG, eG, 1.0, None, ALU.add).then_inc(mdv, 1)
                ve.wait_ge(mdv, 4 * i + 3)
                v.reciprocal(eG, eG).then_inc(mdv, 1)
                ve.wait_ge(mdv, 4 * i + 4)
                tt(hE, eU, eG, ALU.mult).then_inc(hE_ready, 1)
                ve.wait_ge(th_full, i + 1)
                v.tensor_copy(hET, banks[3][:, :].rearrange("p (k t) -> p k t", k=4)).then_inc(hT_cp, 1)

            moe_loops(ve, pair_of_blocks)
            for t in range(NT + 1):
                if t < NT:
                    rows = TILES[t][1]
                    o = fin[t % 3][0:rows, :]
                    ve.wait_ge(yg_ld[t], 32)
                    if t >= 3:
                        ve.wait_ge(fin_st[t % 3], 16)
                    n.link(stt(out=o, in0=yg[t][0][0:rows, :], scalar=gate[0][0:rows, t:t + 1], in1=x_sb[0:rows, t, :],
                               op0=ALU.mult, op1=ALU.add))
                    stt(out=o, in0=yg[t][1][0:rows, :], scalar=gate[1][0:rows, t:t + 1], in1=o,
                        op0=ALU.mult, op1=ALU.add).then_inc(fsum, 1)
                if t >= 1:
                    rows = TILES[t - 1][1]
                    o = fin[(t - 1) % 3][0:rows, :]
                    ve.wait_ge(frstd, t)
                    stt(out=o, in0=o, scalar=rstd[0:rows, 16 + t:17 + t], in1=gfin[0:rows, :], op0=ALU.mult,
                        op1=ALU.mult).then_inc(fin_ready, 1)


_INS = ["x_prompt", "x_sample", "mem_prompt", "cache_diff_k", "cache_diff_v", "state_hgrn", "cache_mem_k", "cache_mem_v",
        "ln_mix_g", "w_in", "da_lambda", "da_subln_g", "hg_lb_logits", "hg_gnorm_g", "w_out", "ln_mem_g", "mem_norm_g",
        "w_mem_q", "w_mem_k", "w_mem_v", "w_mem_o", "ln_ffn_g", "router_group_w", "router_group_b", "router_expert_w",
        "router_expert_b", "exp_w_gate", "exp_w_up", "exp_w_down", "final_norm_g"]
_OUTS = [(1, 512, 1024), (1, 64, 1024), (1, 1, 512, 4, 128), (1, 1, 512, 4, 128), (1, 1, 4, 128, 128),
         (1, 1, 256, 4, 256), (1, 1, 256, 4, 256), (1, 1, 64, 4, 128), (1, 1, 64, 4, 128), (1, 1, 4, 128, 128)]


def kernel(**inputs):
    import numpy as _np
    import concourse.bacc as _bacc
    from concourse import mybir as _mybir
    from concourse.bass_utils import run_bass_kernel_spmd as _run

    nc = _bacc.Bacc("TRN2", target_bir_lowering=False, num_devices=1)
    arrays, args, outs = {}, {}, []
    for name in _INS:
        x = _np.ascontiguousarray(inputs[name])
        arrays[f"in_{name}_dram"] = x
        args[name] = nc.dram_tensor(f"in_{name}_dram", x.shape, _mybir.dt.from_np(x.dtype), kind="ExternalInput").ap()
    for i, shape in enumerate(_OUTS):
        outs.append(nc.dram_tensor(f"out_{i}_dram", shape, _mybir.dt.float32, kind="ExternalOutput").ap())
    encoder(nc, args, outs)
    r = _run(nc, [arrays], core_ids=[0])
    return tuple(r.results[0][f"out_{i}_dram"] for i in range(len(_OUTS)))
```
